# Optimizing a Trainium2 kernel written in Bass

```python
import math
import jax, jax.numpy as jnp
from jax import lax
import numpy as np

D_MODEL = 1024
BATCH = 1
SEQ = 256
DEPTH = 2

CONV_CH = D_MODEL // 2
CONV_KERNEL = 31
HEAD_DIM = 64
N_HEADS = (D_MODEL // 2) // HEAD_DIM
ATTN_WIDTH = N_HEADS * HEAD_DIM
MOBA_BLOCK = 256
MOBA_TOPK = 3
Q_CHUNK = 128
NUM_BUCKETS = 32
MAX_DISTANCE = 2048
D_FF = ((int(8 * D_MODEL / 3) + 255) // 256) * 256
FFN_CONV = 3
EPS = 1e-6
IN_WIDTH = 2 * CONV_CH + 3 * ATTN_WIDTH + 2 * D_MODEL
IN_SPLITS = (CONV_CH, 2 * CONV_CH, 2 * CONV_CH + ATTN_WIDTH, 2 * CONV_CH + 2 * ATTN_WIDTH,
             2 * CONV_CH + 3 * ATTN_WIDTH, 2 * CONV_CH + 3 * ATTN_WIDTH + D_MODEL)

kernel_name = "hybrid_conformer_moba_gated_trunk"

def rmsnorm(x, g):
    xf = x.astype(jnp.float32)
    y = xf * lax.rsqrt(jnp.mean(xf * xf, axis=-1, keepdims=True) + EPS)
    return (y * g.astype(jnp.float32)).astype(x.dtype)

def layernorm(x, g, b):
    xf = x.astype(jnp.float32)
    mu = jnp.mean(xf, axis=-1, keepdims=True)
    var = jnp.mean(jnp.square(xf - mu), axis=-1, keepdims=True)
    y = (xf - mu) * lax.rsqrt(var + EPS)
    return (y * g.astype(jnp.float32) + b.astype(jnp.float32)).astype(x.dtype)

def causal_dwconv(x, w, b):
    width = w.shape[0]
    y = lax.conv_general_dilated(
        x, w[:, None, :].astype(x.dtype), window_strides=(1,), padding=((width - 1, 0),),
        dimension_numbers=("NWC", "WIO", "NWC"), feature_group_count=x.shape[-1])
    return y + b.astype(x.dtype)

def t5_bucket(dist):
    dist = jnp.maximum(dist, 0)
    max_exact = NUM_BUCKETS // 2
    nf = jnp.maximum(dist, 1).astype(jnp.float32)
    large = max_exact + (jnp.log(nf / max_exact) / math.log(MAX_DISTANCE / max_exact)
                         * (NUM_BUCKETS - max_exact)).astype(jnp.int32)
    large = jnp.minimum(large, NUM_BUCKETS - 1)
    return jnp.where(dist < max_exact, dist, large)

def moba_attention(q, k, v, rel_bias):
    bsz, nh, S, hd = q.shape
    nb = -(-S // MOBA_BLOCK)
    s_pad = nb * MOBA_BLOCK
    pad = ((0, 0), (0, 0), (0, s_pad - S), (0, 0))
    kb = jnp.pad(k, pad).reshape(bsz, nh, nb, MOBA_BLOCK, hd)
    vb = jnp.pad(v, pad).reshape(bsz, nh, nb, MOBA_BLOCK, hd)
    k_mean = jnp.mean(kb.astype(jnp.float32), axis=3)
    pos = jnp.arange(S, dtype=jnp.int32)
    own = pos // MOBA_BLOCK
    gate = jnp.einsum("bhsd,bhnd->bhsn", q.astype(jnp.float32), k_mean)
    fully_past = jnp.arange(nb, dtype=jnp.int32)[None, :] < own[:, None]
    gate = jnp.where(fully_past, gate, -jnp.inf)
    k_sel = min(MOBA_TOPK, nb)
    _, top_idx = lax.top_k(gate, k_sel)
    top_idx = top_idx.astype(jnp.int32)
    sel_valid = top_idx < own[:, None]
    own_b = jnp.broadcast_to(own[:, None], (bsz, nh, S, 1))
    blocks = jnp.concatenate([top_idx, own_b], axis=-1)
    valid = jnp.concatenate([sel_valid, jnp.ones((bsz, nh, S, 1), bool)], axis=-1)
    n_sel = k_sel + 1
    scale = HEAD_DIM ** -0.5
    b_ix = jnp.arange(bsz)[:, None, None, None]
    h_ix = jnp.arange(nh)[None, :, None, None]
    h_ix5 = h_ix[..., None]
    in_block = jnp.arange(MOBA_BLOCK, dtype=jnp.int32)

    def one_chunk(ci):
        start = ci * Q_CHUNK
        qc = lax.dynamic_slice_in_dim(q, start, Q_CHUNK, axis=2)
        bc = lax.dynamic_slice_in_dim(blocks, start, Q_CHUNK, axis=2)
        vc = lax.dynamic_slice_in_dim(valid, start, Q_CHUNK, axis=2)
        qpos = start + jnp.arange(Q_CHUNK, dtype=jnp.int32)
        kg = kb[b_ix, h_ix, bc]
        vg = vb[b_ix, h_ix, bc]
        kpos = bc[..., None] * MOBA_BLOCK + in_block
        dist = qpos[:, None, None] - kpos
        logits = jnp.einsum("bhqd,bhqnkd->bhqnk", qc, kg,
                            preferred_element_type=jnp.float32) * scale
        logits = logits + rel_bias[h_ix5, t5_bucket(dist)].astype(jnp.float32)
        mask = vc[..., None] & (dist >= 0)
        logits = jnp.where(mask, logits, -jnp.inf)
        p = jax.nn.softmax(logits.reshape(bsz, nh, Q_CHUNK, n_sel * MOBA_BLOCK), axis=-1)
        p = p.reshape(bsz, nh, Q_CHUNK, n_sel, MOBA_BLOCK).astype(v.dtype)
        return jnp.einsum("bhqnk,bhqnkd->bhqd", p, vg)

    out = lax.map(one_chunk, jnp.arange(S // Q_CHUNK, dtype=jnp.int32))
    return jnp.moveaxis(out, 0, 2).reshape(bsz, nh, S, hd)

def mixer(h, w_in, conv_w, conv_b, conv_ln_g, conv_ln_b, q_norm_g, k_norm_g,
          w_pa, w_pb, w_o, rel_bias):
    bsz, S, _ = h.shape
    z = h @ w_in
    cv, cg, q, k, v, ga, gb = jnp.split(z, IN_SPLITS, axis=-1)
    a = cv * jax.nn.sigmoid(cg)
    a = causal_dwconv(a, conv_w, conv_b)
    a = jax.nn.silu(layernorm(a, conv_ln_g, conv_ln_b))
    ya = a @ w_pa
    q = rmsnorm(q.reshape(bsz, S, N_HEADS, HEAD_DIM), q_norm_g).transpose(0, 2, 1, 3)
    k = rmsnorm(k.reshape(bsz, S, N_HEADS, HEAD_DIM), k_norm_g).transpose(0, 2, 1, 3)
    v = v.reshape(bsz, S, N_HEADS, HEAD_DIM).transpose(0, 2, 1, 3)
    o = moba_attention(q, k, v, rel_bias)
    yb = o.transpose(0, 2, 1, 3).reshape(bsz, S, ATTN_WIDTH) @ w_pb
    m = jax.nn.sigmoid(ga) * ya + jax.nn.sigmoid(gb) * yb
    return m @ w_o

def conv_ffn(h, w_up, ffn_conv_w, ffn_conv_b, w_down):
    u = causal_dwconv(h @ w_up, ffn_conv_w, ffn_conv_b)
    uv, ug = jnp.split(u, 2, axis=-1)
    return (jax.nn.silu(ug) * uv) @ w_down

def setup_inputs(seed: int = 0) -> dict:
    key = jax.random.key(seed)
    ks = jax.random.split(key, 24)
    f32 = jnp.float32

    def nrm(k, shape, scale):
        return jax.random.normal(k, shape, f32) * scale

    L, D, C, A, F = DEPTH, D_MODEL, CONV_CH, ATTN_WIDTH, D_FF
    return {
        "x": nrm(ks[0], (BATCH, SEQ, D), 1.0),
        "c": nrm(ks[1], (BATCH, D), 1.0),
        "ada_w": nrm(ks[2], (L, D, 6 * D), 0.5 * D ** -0.5),
        "ada_b": nrm(ks[3], (L, 6 * D), 0.02),
        "norm1_g": 1.0 + nrm(ks[4], (L, D), 0.05),
        "w_in": nrm(ks[5], (L, D, IN_WIDTH), D ** -0.5),
        "conv_w": nrm(ks[6], (L, CONV_KERNEL, C), CONV_KERNEL ** -0.5),
        "conv_b": nrm(ks[7], (L, C), 0.02),
        "conv_ln_g": 1.0 + nrm(ks[8], (L, C), 0.05),
        "conv_ln_b": nrm(ks[9], (L, C), 0.02),
        "q_norm_g": 1.0 + nrm(ks[10], (L, HEAD_DIM), 0.05),
        "k_norm_g": 1.0 + nrm(ks[11], (L, HEAD_DIM), 0.05),
        "w_pa": nrm(ks[12], (L, C, D), C ** -0.5),
        "w_pb": nrm(ks[13], (L, A, D), A ** -0.5),
        "w_o": nrm(ks[14], (L, D, D), D ** -0.5),
        "norm2_g": 1.0 + nrm(ks[15], (L, D), 0.05),
        "w_up": nrm(ks[16], (L, D, 2 * F), D ** -0.5),
        "ffn_conv_w": nrm(ks[17], (L, FFN_CONV, 2 * F), FFN_CONV ** -0.5),
        "ffn_conv_b": nrm(ks[18], (L, 2 * F), 0.02),
        "w_down": nrm(ks[19], (L, F, D), F ** -0.5),
        "rel_bias": nrm(ks[20], (N_HEADS, NUM_BUCKETS), 0.5),
    }

def reference(x, c, ada_w, ada_b, norm1_g, w_in, conv_w, conv_b, conv_ln_g, conv_ln_b,
              q_norm_g, k_norm_g, w_pa, w_pb, w_o, norm2_g, w_up, ffn_conv_w, ffn_conv_b,
              w_down, rel_bias):
    cond = jax.nn.silu(c)
    for l in range(DEPTH):
        mod = (cond @ ada_w[l] + ada_b[l])[:, None, :]
        sh1, sc1, g1, sh2, sc2, g2 = jnp.split(mod, 6, axis=-1)
        h = rmsnorm(x, norm1_g[l]) * (1.0 + sc1) + sh1
        x = x + g1 * mixer(h, w_in[l], conv_w[l], conv_b[l], conv_ln_g[l], conv_ln_b[l],
                           q_norm_g[l], k_norm_g[l], w_pa[l], w_pb[l], w_o[l], rel_bias)
        h = rmsnorm(x, norm2_g[l]) * (1.0 + sc2) + sh2
        x = x + g2 * conv_ffn(h, w_up[l], ffn_conv_w[l], ffn_conv_b[l], w_down[l])
    return x


_drawn_inputs = setup_inputs


def setup_inputs(seed=0):
    import zlib

    import numpy as np

    out = dict(_drawn_inputs(seed))
    spreads = {}
    factors = {'norm1_g': 5.975,
     'conv_b': 8.0,
     'conv_ln_g': 7.045,
     'conv_ln_b': 8.0,
     'q_norm_g': 8.0,
     'k_norm_g': 8.0,
     'ffn_conv_b': 7.095,
     'rel_bias': 2.958}
    for name, (base, spread) in spreads.items():
        noise = np.random.default_rng([zlib.crc32(name.encode()), seed]).standard_normal(out[name].shape)
        drawn = base * np.exp(spread * noise) if base else spread * noise
        out[name] = __import__('jax').numpy.asarray(drawn.astype(out[name].dtype))
    for name, factor in factors.items():
        out[name] = (out[name] * factor).astype(out[name].dtype)
    return out
```

```python
import math
from contextlib import ExitStack

import numpy as np

import concourse.bass as bass
from concourse import mybir

F32 = mybir.dt.float32
F32R = mybir.dt.float32r
BF16 = mybir.dt.bfloat16
ALU = mybir.AluOpType
ACT = mybir.ActivationFunctionType
AX = mybir.AxisListType

P = 128
D = 1024
T = 256
DEPTH = 2
CONV_CH = D // 2
TAPS = 31
HD = 64
HEADS = (D // 2) // HD
BUCKETS = 32
MAX_DISTANCE = 2048
D_FF = ((int(8 * D / 3) + 255) // 256) * 256
FTAPS = 3
EPS = 1e-6
KD = D // P
KC = CONV_CH // P
TT = T // P
PAIRS = D_FF // (2 * P)
KF = 2 * D_FF // P
CH = 2048
MASKED = -1.0e30

N_CONV = 0
N_QKV = 4
N_GATE = 10
N_PA = 18
N_PB = 20
N_WO = 22
N_FFN = 26
N_SPLIT = N_FFN + 3 * PAIRS
ADA_GROUPS = 6 * D // 512
ADA_FIRST = 4
N_ADA = 2 * ADA_GROUPS
RAW_SLOTS = 6
SPLIT_SLOTS = 3
LOOKAHEAD = 2


def ada_group_after(n):
    if N_QKV <= n and (n - N_QKV) % 2 == 0 and ADA_FIRST + (n - N_QKV) // 2 < ADA_GROUPS:
        return ADA_FIRST + (n - N_QKV) // 2
    return None


def stream_order():
    order = [("ada", a) for a in range(2 * ADA_FIRST)]
    for n in range(N_SPLIT):
        order.append(("split", n))
        g = ada_group_after(n)
        if g is not None:
            order += [("ada", 2 * g), ("ada", 2 * g + 1)]
    return order


ORDER = stream_order()
N_RAW = len(ORDER)
RAW_OF = {what: r for r, what in enumerate(ORDER)}
USES = [sum(r % RAW_SLOTS == s for r in range(N_RAW)) for s in range(RAW_SLOTS)]

V_G1 = 0
V_G2 = V_G1 + KD
V_CW = V_G2 + KD
V_CB = V_CW + TAPS * KC
V_LG = V_CB + KC
V_LB = V_LG + KC
V_QG = V_LB + KC
V_KG = V_QG + 1
V_FW = V_KG + 1
V_FB = V_FW + FTAPS * KF
V_AB = V_FB + KF
NV = V_AB + 6 * KD
M_SH1, M_SC1, M_GA1, M_SH2, M_SC2, M_GA2 = (KD * i for i in range(6))

TABLE = 2 * T - P - 1
CONV_OPS = [(tap, t) for tap in range(TAPS) for t in range(KC)]
CONV_STEPS = range(N_QKV, 16)


def conv_share(n):
    if n not in CONV_STEPS:
        return []
    at, of = n - CONV_STEPS[0], len(CONV_STEPS)
    return list(range(len(CONV_OPS) * at // of, len(CONV_OPS) * (at + 1) // of))


def trunk(nc, stream, x_in, c_in, packs_in, rel_in, onehot_in, ident_in, flip_in, out):
    ctx = ExitStack()
    with ctx:
        def sb(name, shape, dt=F32):
            return ctx.enter_context(nc.sbuf_tensor(name, shape, dt))

        def sem(name):
            return ctx.enter_context(nc.semaphore(name))

        raw = [sb(f"raw{i}", [P, CH]) for i in range(RAW_SLOTS)]
        w_hi = [sb(f"w_hi{i}", [P, CH], F32R) for i in range(SPLIT_SLOTS)]
        w_lo = [sb(f"w_lo{i}", [P, CH], F32R) for i in range(SPLIT_SLOTS)]
        x = sb("x", [P, KD, T])
        h_hi = sb("h_hi", [P, KD, T], F32R)
        h_lo = sb("h_lo", [P, KD, T], F32R)
        work = sb("work", [P, KD, T])
        q_tok = work[:, 0:4, :].rearrange("p (a b) t -> p a (b t)", a=TT)
        k_tok = work[:, 4:8, :].rearrange("p (a b) t -> p a (b t)", a=TT)
        gates = sb("gates", [P, 2 * KD, T])
        ada_rows_a = gates[:, 0:8, :].rearrange("p (a b) t -> p a (b t)", a=ADA_FIRST)
        ada_rows_b = sb("ada_rows_b", [P, 512])
        glu = sb("glu", [P, KC, TAPS - 1 + T])
        acc = sb("acc", [P, KC, T])
        lin = sb("lin", [P, KC, T])
        a_hi = sb("a_hi", [P, KC, T], F32R)
        a_lo = sb("a_lo", [P, KC, T], F32R)
        v_tok = sb("v_tok", [P, TT, 512])
        qT = sb("qT", [P, KC, T])
        kT = sb("kT", [P, KC, T])
        bias = sb("bias", [P, HEADS, T])
        probs = sb("probs", [P, 2, 3 * P])
        pT = sb("pT", [P, 2, 3 * P])
        o_tok = q_tok
        u = gates[:, 0:4, :]
        f_hi = a_hi[:, :, :].rearrange("p (a b) t -> p a b t", a=2)
        f_lo = a_lo[:, :, :].rearrange("p (a b) t -> p a b t", a=2)
        packs = sb("packs", [P, DEPTH, NV])
        vec = sb("vec", [P, NV])
        mod = sb("mod", [P, 6 * KD])
        gs = sb("gs", [P, 2, KD])
        qg8 = sb("qg8", [P, 1])
        cT = sb("cT", [P, KD])
        cond = sb("cond", [P, KD, 32])
        ident = sb("ident", [P, P])
        flip = sb("flip", [P, P])
        ones = sb("ones", [P, P])
        zeros = sb("zeros", [P, 512], BF16)
        neg_half = sb("neg_half", [P, 16])
        stat = sb("stat", [P, TT])
        rstd = sb("rstd", [P, TT])
        diag = sb("diag", [P, TT, P])
        qk_stat = sb("qk_stat", [P, 2, TT * HEADS])
        qk_rstd = sb("qk_rstd", [P, 2, TT * HEADS])
        row_max = sb("row_max", [P, HEADS, TT])
        row_sum = sb("row_sum", [P, HEADS, TT])
        row_inv = sb("row_inv", [P, HEADS, TT])
        onehot = sb("onehot", [BUCKETS + 1, TABLE])
        rel = sb("rel", [BUCKETS + 1, HEADS])
        table = sb("table", [HEADS, TABLE])
        table_dram = nc.dram_tensor("table_scratch", (HEADS, TABLE), F32, kind="Internal").ap()

        bank = [ctx.enter_context(nc.psum_tensor(f"bank{i}", [P, 512], F32)) for i in range(8)]

        raw_full = [sem(f"raw_full{i}") for i in range(RAW_SLOTS)]
        hi_done = sem("hi_done")
        lo_done = sem("lo_done")
        used = sem("used")
        ada_used = sem("ada_used")
        row_ev = sem("row_ev")
        modt = sem("modt")
        mod_done = sem("mod_done")
        vec_done = sem("vec_done")
        gs_done = sem("gs_done")
        sq_done = sem("sq_done")
        stat_mm = sem("stat_mm")
        stat_ev = sem("stat_ev")
        rstd_done = sem("rstd_done")
        diag_done = sem("diag_done")
        bcast = sem("bcast")
        xn_done = sem("xn_done")
        hi_h = sem("hi_h")
        aff_h = sem("aff_h")
        lo_h = sem("lo_h")
        cg_sig = sem("cg_sig")
        glu_done = sem("glu_done")
        conv = sem("conv")
        mean_mm = sem("mean_mm")
        cen_done = sem("cen_done")
        cn_done = sem("cn_done")
        ln_sig = sem("ln_sig")
        ln_aff = sem("ln_aff")
        a_done = sem("a_done")
        a_hi_done = sem("a_hi_done")
        a_lo_done = sem("a_lo_done")
        qk_sq = sem("qk_sq")
        qk_red = sem("qk_red")
        qk_mean = sem("qk_mean")
        qk_pow = sem("qk_pow")
        qk_norm = sem("qk_norm")
        qk_tr = sem("qk_tr")
        qk_ev = sem("qk_ev")
        v_ev = sem("v_ev")
        gate_ev = sem("gate_ev")
        gate_sig = sem("gate_sig")
        s_mm = sem("s_mm")
        s_ev = sem("s_ev")
        max_done = sem("max_done")
        max_raw = sem("max_raw")
        exp_done = sem("exp_done")
        inv_done = sem("inv_done")
        pt_mm = sem("pt_mm")
        pt_ev = sem("pt_ev")
        o_tr = sem("o_tr")
        o_hi_done = sem("o_hi_done")
        o_lo_done = sem("o_lo_done")
        pa_ev = sem("pa_ev")
        pb_ev = sem("pb_ev")
        m_done = sem("m_done")
        m_hi_done = sem("m_hi_done")
        m_lo_done = sem("m_lo_done")
        x_upd = sem("x_upd")
        u_ev = sem("u_ev")
        u_conv = sem("u_conv")
        u_silu = sem("u_silu")
        f_done = sem("f_done")
        f_hi_done = sem("f_hi_done")
        f_lo_done = sem("f_lo_done")
        ld_small = [sem(f"ld_small{i}") for i in range(7)]
        const_done = sem("const_done")
        cond_done = sem("cond_done")
        rel_done = sem("rel_done")
        table_mm = sem("table_mm")
        table_ev = sem("table_ev")
        table_out = sem("table_out")
        bias_in = sem("bias_in")
        bias_mm = sem("bias_mm")
        bias_done = sem("bias_done")
        stored = sem("stored")

        def raw_need(L, r, uses_more=0):
            return L * (16 * USES[r % RAW_SLOTS]) + (16 * (r // RAW_SLOTS + 1) + 16 * uses_more)

        block = ctx.enter_context(nc.Block())

        @block.sync
        def _(sp):
            def load(L, r, slot, wait=True, it=0):
                if wait:
                    before = r - RAW_SLOTS
                    if before < 0:
                        before = max(q for q in range(N_RAW) if q % RAW_SLOTS == slot)
                        lower = N_SPLIT
                    else:
                        lower = 0
                    kind, n = ORDER[before]
                    if kind == "split":
                        sp.wait_ge(lo_done, L * N_SPLIT + it * RAW_SLOTS + (n + 1 - lower + RAW_SLOTS))
                    else:
                        sp.wait_ge(ada_used, L * N_ADA + (n + 1))
                src = stream[L * N_RAW + it * RAW_SLOTS + r, :, :]
                sp.dma_start(raw[slot][:, :], src).then_inc(raw_full[slot], 16)

            sp.dma_start(x[:, :, :], x_in).then_inc(ld_small[0], 16)
            sp.dma_start(cT[:, :], c_in).then_inc(ld_small[1], 16)
            sp.dma_start(packs[:, :, :], packs_in).then_inc(ld_small[2], 16)
            with sp.Fori(0, DEPTH) as L:
                r_loop = RAW_OF[("split", N_FFN + 2)]
                for r in range(r_loop):
                    load(L, r, r % RAW_SLOTS)
                with sp.Fori(0, (PAIRS - 1) // 2) as it:
                    for j in range(RAW_SLOTS):
                        load(L, r_loop + j, (r_loop + j) % RAW_SLOTS, it=it)
                load(L, N_RAW - 1, (N_RAW - 1) % RAW_SLOTS)
            sp.wait_ge(x_upd, DEPTH * 2 * KD + 1)
            sp.dma_start(out, x[:, :, :]).then_inc(stored, 16)
            sp.wait_ge(stored, 16)

        @block.gpsimd
        def _(pool):
            nc.gpsimd.memset(ones[:, :], 1.0)
            nc.gpsimd.memset(neg_half[:, :], -0.5)
            nc.gpsimd.memset(zeros[:, :], 0.0)
            nc.gpsimd.memset(glu[:, :, 0:TAPS - 1], 0.0)
            nc.gpsimd.memset(cond[:, :, :], 0.0).then_inc(const_done, 1)
            pool.wait_ge(ld_small[2], 16)
            with pool.Fori(0, DEPTH) as L:
                pool.wait_ge(x_upd, L * (2 * KD) + 1)
                nc.gpsimd.tensor_copy(vec[:, :], packs[:, L, :]).then_inc(vec_done, 1)

                def power(i):
                    pool.wait_ge(stat_ev, L * 3 + (i + 1))
                    nc.gpsimd.tensor_tensor(rstd[:, :], stat[:, :], neg_half[:, 0:TT],
                                            ALU.pow).then_inc(rstd_done, 1)

                power(0)
                for m in range(2):
                    pool.wait_ge(qk_mean, L * 2 + (m + 1))
                    nc.gpsimd.tensor_tensor(qk_rstd[:, m, :], qk_stat[:, m, :], neg_half[:, :],
                                            ALU.pow).then_inc(qk_pow, 1)
                power(1)
                power(2)

        @block.scalar
        def _(act):
            act.dma_start(ident[:, :], ident_in).then_inc(ld_small[3], 16)
            act.dma_start(rel[0:BUCKETS, :], rel_in).then_inc(ld_small[4], 16)
            act.dma_start(onehot[:, :], onehot_in).then_inc(ld_small[5], 16)
            act.dma_start(flip[:, :], flip_in).then_inc(ld_small[6], 16)
            act.wait_ge(ld_small[1], 16)
            act.wait_ge(const_done, 1)
            nc.scalar.activation(cond[:, :, 0], cT[:, :], ACT.Silu).then_inc(cond_done, 1)
            act.wait_ge(table_ev, 1)
            act.dma_start(table_dram, table[:, :]).then_inc(table_out, 16)
            act.wait_ge(table_out, 16)
            for i, part in enumerate((acc, lin)):
                src = bass.AP(tensor=table_dram.tensor, offset=4 * i * TABLE, ap=[[1, P], [TABLE, 4], [1, T]])
                act.dma_start(part[:, :, :], src).then_inc(bias_in, 16)
            act.wait_ge(ld_small[0], 16)
            with act.Fori(0, DEPTH) as L:
                def split(n, slot=None, it=0):
                    slot = n % SPLIT_SLOTS
                    r = RAW_OF[("split", n)]
                    act.wait_ge(raw_full[r % RAW_SLOTS], raw_need(L, r, it))
                    if n >= SPLIT_SLOTS:
                        act.wait_ge(used, L * N_SPLIT + it * RAW_SLOTS + (n + 1 - SPLIT_SLOTS))
                    else:
                        act.wait_ge(vec_done, L + 1)
                    nc.scalar.activation(w_hi[slot][:, :], raw[r % RAW_SLOTS][:, :],
                                         ACT.Copy).then_inc(hi_done, 1)

                def rows(g):
                    act.wait_ge(ada_used, L * N_ADA + 2 * (g + 1))
                    if g < ADA_FIRST:
                        dst, src = ada_rows_a[:, g, :], bank[g]
                    else:
                        act.wait_ge(modt, L * ADA_GROUPS + g)
                        dst, src = ada_rows_b[:, :], bank[7]
                    nc.scalar.activation(dst, src[:, :], ACT.Copy).then_inc(row_ev, 1)

                def squares(i):
                    act.wait_ge(x_upd, L * (2 * KD) + (i * KD + 1))
                    nc.scalar.activation(work[:, :, :], x[:, :, :], ACT.Square).then_inc(sq_done, 1)

                def high_h(i):
                    act.wait_ge(gs_done, L * 3 + (1 if i == 0 else 3))
                    for c in range(KD):
                        act.wait_ge(xn_done, L * 8 + i * 4 + c // 2 + 1)
                        shift = (M_SH1 if i == 0 else M_SH2) + c
                        nc.scalar.activation(h_hi[:, c, :], work[:, c, :], ACT.Identity,
                                             bias=mod[:, shift:shift + 1],
                                             scale=gs[:, i, c:c + 1]).then_inc(hi_h, 1)

                squares(0)
                for g in range(ADA_FIRST):
                    rows(g)
                split(0)
                high_h(0)
                split(1)

                def conv_gate(j):
                    act.wait_ge(used, L * N_SPLIT + N_CONV + 2 * j + 2)
                    if j == 0:
                        act.wait_ge(modt, L * ADA_GROUPS + ADA_FIRST)
                    nc.scalar.activation(gates[:, 2 * j:2 * j + 2, :],
                                         bank[2 * j + 1][:, :].rearrange("p (a t) -> p a t", a=2),
                                         ACT.Sigmoid).then_inc(cg_sig, 1)

                def qk_squares(m):
                    act.wait_ge(used, L * N_SPLIT + N_QKV + 2 * m + 2)
                    for tt in range(TT):
                        if m == 1:
                            act.wait_ge(qk_red, L * 2 * TT + tt + 1)
                        nc.scalar.activation(lin[:, 2 * tt:2 * tt + 2, :],
                                             bank[2 * m + tt][:, :].rearrange("p (a t) -> p a t", a=2),
                                             ACT.Square).then_inc(qk_sq, 1)

                def qk_copy(m):
                    if m == 0:
                        act.wait_ge(gs_done, L * 3 + 2)
                    for b in range(2):
                        act.wait_ge(qk_tr, L * 4 + 2 * m + b + 1)
                        dst = (qT if m == 0 else kT)[:, 2 * b:2 * b + 2, :]
                        gain = qg8[:, 0:1] if m == 0 else vec[:, V_KG:V_KG + 1]
                        nc.scalar.activation(dst, bank[4 + b][:, :].rearrange("p (a t) -> p a t", a=2),
                                             ACT.Copy, scale=gain).then_inc(qk_ev, 1)

                def v_copy():
                    act.wait_ge(used, L * N_SPLIT + N_QKV + 6)
                    for tt in range(TT):
                        nc.scalar.activation(v_tok[:, tt, :], bank[tt][:, :], ACT.Copy).then_inc(v_ev, 1)

                def gate_copy(j):
                    act.wait_ge(used, L * N_SPLIT + N_GATE + j + 1)
                    if j == 0:
                        act.wait_ge(glu_done, L * 2 + 2)
                    nc.scalar.activation(gates[:, 2 * j:2 * j + 2, :],
                                         bank[(2 + j) % 4][:, :].rearrange("p (a t) -> p a t", a=2),
                                         ACT.Copy).then_inc(gate_ev, 1)

                def attend(t):
                    if t >= 1:
                        act.wait_ge(pt_mm, L * (HEADS + 1) + t)
                        if t >= 2:
                            hh = t - 2
                            act.wait_ge(inv_done, L * HEADS + hh + 1)
                            for tt in range(TT):
                                last = nc.scalar.activation(
                                    o_tok[:, tt, hh * HD:(hh + 1) * HD],
                                    bank[5][:, 3 * P + tt * HD:3 * P + (tt + 1) * HD],
                                    ACT.Copy, scale=row_inv[:, hh, tt:tt + 1])
                        if t <= HEADS:
                            last = nc.scalar.activation(pT[:, (t - 1) % 2, :], bank[5][:, 0:3 * P], ACT.Copy)
                        last.then_inc(pt_ev, 1)
                    if t < HEADS:
                        act.wait_ge(max_done, L * HEADS + t + 1)
                        nc.scalar.activation(probs[:, t % 2, 0:P], probs[:, t % 2, 0:P], ACT.Exp,
                                             bias=row_max[:, t, 0:1], accum_out=row_sum[:, t, 0:1])
                        nc.scalar.activation(probs[:, t % 2, P:3 * P], probs[:, t % 2, P:3 * P], ACT.Exp,
                                             bias=row_max[:, t, 1:2],
                                             accum_out=row_sum[:, t, 1:2]).then_inc(exp_done, 1)

                def ln_squares():
                    act.wait_ge(cen_done, L + 1)
                    nc.scalar.activation(lin[:, :, :], acc[:, :, :], ACT.Square).then_inc(sq_done, 1)

                def ln_tail():
                    act.wait_ge(cn_done, L + 1)
                    for t in range(KC):
                        nc.scalar.activation(lin[:, t, :], acc[:, t, :], ACT.Sigmoid,
                                             bias=vec[:, V_LB + t:V_LB + t + 1],
                                             scale=vec[:, V_LG + t:V_LG + t + 1]).then_inc(ln_sig, 1)
                    act.wait_ge(a_done, L + 1)
                    nc.scalar.activation(a_hi[:, :, :], acc[:, :, :], ACT.Copy).then_inc(a_hi_done, 1)

                def gate_sigmoids():
                    act.wait_ge(gate_ev, L * 8 + 8)
                    for s in range(2):
                        half = gates[:, s * KD:(s + 1) * KD, :]
                        nc.scalar.activation(half, half, ACT.Sigmoid).then_inc(gate_sig, 1)

                def o_high():
                    for b in range(2):
                        act.wait_ge(o_tr, L * 2 + b + 1)
                        nc.scalar.activation(qT_hi(b), bank[4 + b][:, :].rearrange("p (a t) -> p a t", a=2),
                                             ACT.Copy).then_inc(o_hi_done, 1)

                def m_high(half):
                    act.wait_ge(m_done, L * 2 + half + 1)
                    nc.scalar.activation(h_hi[:, 4 * half:4 * half + 4, :], gates[:, 4 * half:4 * half + 4, :],
                                         ACT.Copy).then_inc(m_hi_done, 1)

                def qT_hi(b):
                    return a_hi[:, 2 * b:2 * b + 2, :]

                for n in range(N_FFN):
                    split(n + LOOKAHEAD)
                    g = ada_group_after(n)
                    if g is not None:
                        rows(g)
                    if n in (N_CONV + 1, N_CONV + 3):
                        conv_gate((n - N_CONV) // 2)
                    if n == N_QKV + 1:
                        qk_squares(0)
                    if n == N_QKV + 3:
                        qk_squares(1)
                        qk_copy(0)
                    if n == N_QKV + 5:
                        v_copy()
                        qk_copy(1)
                    if N_GATE <= n < N_PA:
                        gate_copy(n - N_GATE)
                    if n == 16:
                        ln_squares()
                    if N_GATE <= n < N_GATE + HEADS + 2:
                        attend(n - N_GATE)
                    if n == 17:
                        ln_tail()
                    if n == N_PA:
                        gate_sigmoids()
                    if n == N_PA + 1:
                        o_high()
                    if N_PB <= n < N_WO:
                        m_high(n - N_PB)
                squares(1)
                split(N_FFN + 2)
                high_h(1)
                split(N_FFN + 3)

                def ffn(i, first, parity):
                    for s in range(2):
                        act.wait_ge(used, L * N_SPLIT + (first + s + 1))
                        if s == 0 and not isinstance(i, int) or s == 0 and i > 0:
                            act.wait_ge(f_lo_done, L * PAIRS + i)
                        for t in range(2):
                            col = 2 * i + t + s * (KF // 2)
                            b = bank[2 * parity + s]
                            nc.scalar.activation(u[:, 2 * s + t, :], b[:, t * T:(t + 1) * T], ACT.Identity,
                                                 bias=at(V_FB, col), scale=at(V_FW + 2 * KF, col)).then_inc(u_ev, 1)
                    act.wait_ge(u_conv, L * 8 * PAIRS + i * 8 + 8)
                    nc.scalar.activation(u[:, 2:4, :], u[:, 2:4, :], ACT.Silu).then_inc(u_silu, 1)
                    act.wait_ge(f_done, L * PAIRS + i + 2)
                    nc.scalar.activation(f_hi[:, parity, :, :], u[:, 0:2, :], ACT.Copy).then_inc(f_hi_done, 1)

                def at(base, col):
                    if isinstance(col, int):
                        return vec[:, base + col:base + col + 1]
                    return vec[:, bass.ds(col + base, 1)]

                ffn(0, N_FFN, 0)

                def ffn_round(it, last):
                    for j in range(2):
                        base = N_FFN + 2 + 3 * j
                        split(base + 2, it=it)
                        if last and j == 1:
                            split(base + 3, it=it)
                        else:
                            split(base + 3, it=it)
                            split(base + 4, it=it)
                        i = it * 2 + (1 + j)
                        ffn(i, it * RAW_SLOTS + base, (1 + j) % 2)

                with act.Fori(0, (PAIRS - 1) // 2 - 1) as it:
                    ffn_round(it, False)
                ffn_round((PAIRS - 1) // 2 - 1, True)

        @block.vector
        def _(dve):
            dve.sem_inc(lo_done, RAW_SLOTS)
            dve.sem_inc(f_done, 1)
            dve.wait_ge(ld_small[4], 16)
            nc.vector.memset(rel[BUCKETS:BUCKETS + 1, :], MASKED).then_inc(rel_done, 1)
            dve.wait_ge(table_mm, 1)
            nc.vector.tensor_copy(table[:, :], bank[0][0:HEADS, 0:TABLE]).then_inc(table_ev, 1)
            dve.wait_ge(bias_mm, 1)
            for i in range(4):
                last = nc.vector.tensor_copy(bias[:, 2 * i:2 * i + 2, :],
                                             bank[i][:, :].rearrange("p (a t) -> p a t", a=2))
            last.then_inc(bias_done, 1)
            dve.wait_ge(ld_small[0], 16)
            dve.sem_inc(x_upd, 1)
            dve.wait_ge(ld_small[3], 16)
            with dve.Fori(0, DEPTH) as L:
                def split(n, it=0):
                    slot = n % SPLIT_SLOTS
                    r = RAW_OF[("split", n)]
                    dve.wait_ge(hi_done, L * N_SPLIT + it * RAW_SLOTS + n + 1)
                    nc.vector.tensor_tensor(w_lo[slot][:, :], raw[r % RAW_SLOTS][:, :],
                                            w_hi[slot][:, :].bitcast(F32), ALU.subtract).then_inc(lo_done, 1)

                def mean_square(i, width, b):
                    dve.wait_ge(stat_mm, L * 3 + i + 1)
                    nc.vector.tensor_scalar(stat[:, :], bank[b][:, 256:256 + TT], 1.0 / width, EPS,
                                            ALU.mult, ALU.add).then_inc(stat_ev, 1)

                def diagonal(i):
                    dve.wait_ge(rstd_done, L * 3 + i + 1)
                    for tt in range(TT):
                        last = nc.vector.tensor_scalar(diag[:, tt, :], ident[:, :], rstd[:, tt:tt + 1], None,
                                                       ALU.mult)
                    last.then_inc(diag_done, 1)

                def scale_x(i):
                    dve.wait_ge(bcast, L * 3 + (1 if i == 0 else 3))
                    for c in range(0, KD, 2):
                        nc.vector.tensor_tensor(work[:, c:c + 2, :], x[:, c:c + 2, :],
                                                bank[4][:, 0:T].unsqueeze(1).broadcast_to((P, 2, T)),
                                                ALU.mult).then_inc(xn_done, 1)

                def norm_gain(i):
                    sc = M_SC1 if i == 0 else M_SC2
                    g = V_G1 if i == 0 else V_G2
                    nc.vector.scalar_tensor_tensor(gs[:, i, :], mod[:, sc:sc + KD], 1.0, vec[:, g:g + KD],
                                                   op0=ALU.add, op1=ALU.mult).then_inc(gs_done, 1)

                def low_h(i):
                    shift = M_SH1 if i == 0 else M_SH2
                    for c in range(KD + 1):
                        if c < KD:
                            dve.wait_ge(hi_h, L * 16 + i * 8 + c + 1)
                            nc.vector.tensor_scalar(work[:, c, :], work[:, c, :], gs[:, i, c:c + 1],
                                                    mod[:, shift + c:shift + c + 1],
                                                    ALU.mult, ALU.add).then_inc(aff_h, 1)
                        if c >= 1:
                            dve.wait_ge(aff_h, L * 16 + i * 8 + c)
                            nc.vector.tensor_tensor(h_lo[:, c - 1, :], work[:, c - 1, :],
                                                    h_hi[:, c - 1, :].bitcast(F32),
                                                    ALU.subtract).then_inc(lo_h, 1)

                def mod_columns(g, count, src):
                    dve.wait_ge(modt, L * ADA_GROUPS + g + count)
                    cols = slice(4 * g, 4 * (g + count))
                    ada_b = vec[:, V_AB + cols.start:V_AB + cols.stop]
                    nc.vector.tensor_tensor(mod[:, cols], src, ada_b, ALU.add).then_inc(mod_done, count)

                mean_square(0, D, 4)
                diagonal(0)
                dve.wait_ge(vec_done, L + 1)
                mod_columns(0, ADA_FIRST, bank[6][:, 0:4 * ADA_FIRST])
                dve.wait_ge(mod_done, L * ADA_GROUPS + ADA_FIRST)
                norm_gain(0)
                nc.vector.tensor_scalar(qg8[:, :], vec[:, V_QG:V_QG + 1], HD ** -0.5, None,
                                        ALU.mult).then_inc(gs_done, 1)
                scale_x(0)
                split(0)
                low_h(0)
                split(1)

                def glu_half(j):
                    dve.wait_ge(cg_sig, L * 2 + j + 1)
                    nc.vector.tensor_tensor(glu[:, 2 * j:2 * j + 2, TAPS - 1:],
                                            bank[2 * j][:, :].rearrange("p (a t) -> p a t", a=2),
                                            gates[:, 2 * j:2 * j + 2, :], ALU.mult).then_inc(glu_done, 1)

                def conv_steps(n):
                    for i in conv_share(n):
                        tap, t = CONV_OPS[i]
                        w = vec[:, V_CW + tap * KC + t:V_CW + tap * KC + t + 1]
                        src = glu[:, t, tap:tap + T]
                        if tap == 0:
                            dve.wait_ge(glu_done, L * 2 + t // 2 + 1)
                            nc.vector.tensor_scalar(acc[:, t, :], src, w, vec[:, V_CB + t:V_CB + t + 1],
                                                    ALU.mult, ALU.add).then_inc(conv, 1)
                        else:
                            dve.wait_ge(conv, L * len(CONV_OPS) + i - KC + 1)
                            nc.vector.scalar_tensor_tensor(acc[:, t, :], src, w, acc[:, t, :],
                                                           op0=ALU.mult, op1=ALU.add).then_inc(conv, 1)

                def qk_sums(m):
                    for tt in range(TT):
                        dve.wait_ge(qk_sq, L * 2 * TT + m * TT + tt + 1)
                        nc.vector.reduce_sum(qk_stat[:, m, tt * HEADS:(tt + 1) * HEADS],
                                             lin[:, 2 * tt:2 * tt + 2, :].rearrange("p a (h d) -> p (a h) d", d=HD),
                                             AX.X).then_inc(qk_red, 1)
                    dve.wait_ge(qk_red, L * 2 * TT + (m + 1) * TT)
                    nc.vector.tensor_scalar(qk_stat[:, m, :], qk_stat[:, m, :], 1.0 / HD, EPS,
                                            ALU.mult, ALU.add).then_inc(qk_mean, 1)

                def qk_scale(m):
                    dve.wait_ge(qk_pow, L * 2 + m + 1)
                    for tt in range(TT):
                        dst = (q_tok if m == 0 else k_tok)[:, tt, :]
                        r = qk_rstd[:, m, tt * HEADS:(tt + 1) * HEADS]
                        nc.vector.tensor_tensor(dst.rearrange("p (h d) -> p h d", d=HD),
                                                bank[2 * m + tt][:, :].rearrange("p (h d) -> p h d", d=HD),
                                                r.unsqueeze(2).broadcast_to((P, HEADS, HD)),
                                                ALU.mult).then_inc(qk_norm, 1)

                def scores(t):
                    dve.wait_ge(s_mm, L * HEADS + t + 1)
                    if t >= 2:
                        dve.wait_ge(pt_mm, L * (HEADS + 1) + t - 1)
                    nc.vector.tensor_tensor(probs[:, t % 2, 0:P], bank[4][:, 0:P], bias[:, t, P:2 * P], ALU.add)
                    nc.vector.tensor_tensor(probs[:, t % 2, P:3 * P], bank[4][:, P:3 * P], bias[:, t, :],
                                            ALU.add).then_inc(s_ev, 1)
                    dve.wait_ge(s_ev, L * HEADS + t + 1)
                    nc.vector.reduce_max(row_max[:, t, 0:1], probs[:, t % 2, 0:P], AX.X)
                    nc.vector.reduce_max(row_max[:, t, 1:2], probs[:, t % 2, P:3 * P], AX.X).then_inc(max_raw, 1)
                    dve.wait_ge(max_raw, L * HEADS + t + 1)
                    nc.vector.tensor_scalar(row_max[:, t, :], row_max[:, t, :], -1.0, None,
                                            ALU.mult).then_inc(max_done, 1)

                def inverse(t):
                    dve.wait_ge(exp_done, L * HEADS + t + 1)
                    nc.vector.reciprocal(row_inv[:, t, :], row_sum[:, t, :]).then_inc(inv_done, 1)

                def centre():
                    dve.wait_ge(mean_mm, L + 1)
                    nc.vector.scalar_tensor_tensor(
                        acc[:, :, :], bank[6][:, 0:T].unsqueeze(1).broadcast_to((P, KC, T)),
                        -1.0 / CONV_CH, acc[:, :, :], op0=ALU.mult, op1=ALU.add).then_inc(cen_done, 1)

                def ln_tail():
                    dve.wait_ge(bcast, L * 3 + 2)
                    nc.vector.tensor_tensor(acc[:, :, :], acc[:, :, :],
                                            bank[6][:, 0:T].unsqueeze(1).broadcast_to((P, KC, T)),
                                            ALU.mult).then_inc(cn_done, 1)
                    for t in range(KC):
                        dve.wait_ge(ln_sig, L * KC + t + 1)
                        nc.vector.tensor_scalar(acc[:, t, :], acc[:, t, :], vec[:, V_LG + t:V_LG + t + 1],
                                                vec[:, V_LB + t:V_LB + t + 1],
                                                ALU.mult, ALU.add).then_inc(ln_aff, 1)
                    dve.wait_ge(ln_aff, L * KC + KC)
                    nc.vector.tensor_tensor(acc[:, :, :], acc[:, :, :], lin[:, :, :], ALU.mult).then_inc(a_done, 1)
                    dve.wait_ge(a_hi_done, L + 1)
                    nc.vector.tensor_tensor(a_lo[:, :, :], acc[:, :, :], a_hi[:, :, :].bitcast(F32),
                                            ALU.subtract).then_inc(a_lo_done, 1)

                def merge_a(j):
                    dve.wait_ge(gate_sig, L * 2 + 1)
                    dve.wait_ge(used, L * N_SPLIT + N_PA + j + 1)
                    for b in range(2):
                        g = gates[:, 4 * j + 2 * b:4 * j + 2 * b + 2, :]
                        nc.vector.tensor_tensor(g, bank[(2 + 2 * j + b) % 4][:, :].rearrange("p (a t) -> p a t", a=2),
                                                g, ALU.mult).then_inc(pa_ev, 1)

                def merge_b(j):
                    dve.wait_ge(gate_sig, L * 2 + 2)
                    dve.wait_ge(used, L * N_SPLIT + N_PB + j + 1)
                    for b in range(2):
                        g = gates[:, KD + 4 * j + 2 * b:KD + 4 * j + 2 * b + 2, :]
                        nc.vector.tensor_tensor(g, bank[(2 + 2 * j + b) % 4][:, :].rearrange("p (a t) -> p a t", a=2),
                                                g, ALU.mult).then_inc(pb_ev, 1)
                    dve.wait_ge(pb_ev, L * 4 + 2 * j + 2)
                    lo, hi = gates[:, 4 * j:4 * j + 4, :], gates[:, KD + 4 * j:KD + 4 * j + 4, :]
                    nc.vector.tensor_tensor(lo, lo, hi, ALU.add).then_inc(m_done, 1)
                    dve.wait_ge(m_hi_done, L * 2 + j + 1)
                    nc.vector.tensor_tensor(h_lo[:, 4 * j:4 * j + 4, :], lo,
                                            h_hi[:, 4 * j:4 * j + 4, :].bitcast(F32),
                                            ALU.subtract).then_inc(m_lo_done, 1)

                def o_low():
                    for b in range(2):
                        dve.wait_ge(o_hi_done, L * 2 + b + 1)
                        nc.vector.tensor_tensor(a_lo[:, 2 * b:2 * b + 2, :],
                                                bank[4 + b][:, :].rearrange("p (a t) -> p a t", a=2),
                                                a_hi[:, 2 * b:2 * b + 2, :].bitcast(F32),
                                                ALU.subtract).then_inc(o_lo_done, 1)

                def residual(c, src, gate):
                    nc.vector.scalar_tensor_tensor(x[:, c, :], src, mod[:, gate + c:gate + c + 1], x[:, c, :],
                                                   op0=ALU.mult, op1=ALU.add).then_inc(x_upd, 1)

                for n in range(N_FFN):
                    split(n + LOOKAHEAD)
                    if n >= 1 and ada_group_after(n - 1) is not None:
                        mod_columns(ADA_FIRST + (n - N_QKV) // 2, 1, bank[7][:, 0:4])
                    if n in (N_CONV + 1, N_CONV + 3):
                        glu_half((n - N_CONV) // 2)
                    if n == N_QKV + 1:
                        qk_sums(0)
                    if n == N_QKV + 3:
                        qk_sums(1)
                    conv_steps(n)
                    if n == N_QKV + 1:
                        qk_scale(0)
                    if n == N_QKV + 3:
                        qk_scale(1)
                    if n == 16:
                        centre()
                    if N_GATE <= n < N_GATE + HEADS:
                        scores(n - N_GATE)
                    if N_GATE < n <= N_GATE + HEADS:
                        inverse(n - N_GATE - 1)
                    if n == 17:
                        mean_square(1, CONV_CH, 6)
                        diagonal(1)
                        ln_tail()
                    if N_PA <= n < N_PB:
                        merge_a(n - N_PA)
                    if n == N_PA + 1:
                        o_low()
                    if N_PB <= n < N_WO:
                        merge_b(n - N_PB)
                    if N_WO <= n < N_FFN:
                        if n == N_WO:
                            dve.wait_ge(mod_done, L * ADA_GROUPS + ADA_GROUPS)
                            norm_gain(1)
                        dve.wait_ge(used, L * N_SPLIT + n + 1)
                        for t in range(2):
                            residual(2 * (n - N_WO) + t, bank[(2 + n - N_WO) % 4][:, t * T:(t + 1) * T], M_GA1)
                mean_square(2, D, 4)
                diagonal(2)
                split(N_FFN + 2)
                scale_x(1)
                low_h(1)
                split(N_FFN + 3)

                def at(base, col):
                    if isinstance(col, int):
                        return vec[:, base + col:base + col + 1]
                    return vec[:, bass.ds(col + base, 1)]

                def ffn(i, parity):
                    done = 0
                    for tap in (1, 0):
                        back = 2 - tap
                        for s in range(2):
                            for t in range(2):
                                if tap == 1:
                                    dve.wait_ge(u_ev, L * 4 * PAIRS + i * 4 + 2 * s + 2)
                                else:
                                    dve.wait_ge(u_conv, L * 8 * PAIRS + i * 8 + done - 3)
                                col = 2 * i + t + s * (KF // 2)
                                dst = u[:, 2 * s + t, back:T]
                                nc.vector.scalar_tensor_tensor(
                                    dst, bank[2 * parity + s][:, t * T:(t + 1) * T - back],
                                    at(V_FW + tap * KF, col), dst,
                                    op0=ALU.mult, op1=ALU.add).then_inc(u_conv, 1)
                                done += 1
                    dve.wait_ge(u_silu, L * PAIRS + i + 1)
                    nc.vector.tensor_tensor(u[:, 0:2, :], u[:, 0:2, :], u[:, 2:4, :], ALU.mult).then_inc(f_done, 1)
                    dve.wait_ge(f_hi_done, L * PAIRS + i + 1)
                    nc.vector.tensor_tensor(f_lo[:, parity, :, :], u[:, 0:2, :],
                                            f_hi[:, parity, :, :].bitcast(F32), ALU.subtract).then_inc(f_lo_done, 1)

                ffn(0, 0)

                def ffn_round(it, last):
                    for j in range(2):
                        base = N_FFN + 2 + 3 * j
                        split(base + 2, it=it)
                        split(base + 3, it=it)
                        if not (last and j == 1):
                            split(base + 4, it=it)
                        ffn(it * 2 + (1 + j), (1 + j) % 2)

                with dve.Fori(0, (PAIRS - 1) // 2 - 1) as it:
                    ffn_round(it, False)
                ffn_round((PAIRS - 1) // 2 - 1, True)
                dve.wait_ge(used, L * N_SPLIT + N_SPLIT)
                for c in range(KD):
                    residual(c, bank[4 + c // 2][:, (c % 2) * T:(c % 2 + 1) * T], M_GA2)

        @block.tensor
        def _(pe):
            pe.wait_ge(ld_small[5], 16)
            pe.wait_ge(rel_done, 1)
            nc.tensor.matmul(bank[0][0:HEADS, 0:TABLE], rel[:, :], onehot[:, :], start=True,
                             stop=True).then_inc(table_mm, 1)
            pe.wait_ge(table_ev, 1)
            pe.wait_ge(cond_done, 1)
            pe.wait_ge(ld_small[3], 16)
            pe.wait_ge(ld_small[6], 16)
            pe.wait_ge(bias_in, 32)
            for i in range(4):
                part = (acc, lin)[i // 2][:, 2 * (i % 2):2 * (i % 2) + 2, :]
                last = nc.tensor.matmul(bank[i][:, :], flip[:, :], part.rearrange("p a t -> p (a t)"),
                                        start=True, stop=True)
            last.then_inc(bias_mm, 1)
            pe.wait_ge(bias_done, 1)
            with pe.Fori(0, DEPTH) as L:
                def three(dst, lo_slot, hi_slot, cols, a_hi_, a_lo_, first, last, check=True):
                    nc.tensor.matmul(dst, hi_slot[:, cols], a_hi_, start=first, stop=False,
                                     skip_group_check=not check)
                    nc.tensor.matmul(dst, hi_slot[:, cols], a_lo_, start=False, stop=False,
                                     skip_group_check=not check)
                    return nc.tensor.matmul(dst, lo_slot[:, cols], a_hi_, start=False, stop=last,
                                            skip_group_check=not check)

                def chunk(n, banks, a_hi_, a_lo_, ks, each=None):
                    slot = n % SPLIT_SLOTS
                    width = CH // ks
                    pe.wait_ge(lo_done, L * N_SPLIT + n + 1 + RAW_SLOTS)
                    for t in range(width // P):
                        for k in range(ks):
                            if each and t == 0:
                                each(k)
                            col = k * width + t * P
                            last = three(bank[banks[t // 2]][:, (t % 2) * T:(t % 2 + 1) * T], w_lo[slot],
                                         w_hi[slot], slice(col, col + P), a_hi_[:, k, :], a_lo_[:, k, :],
                                         k == 0, k == ks - 1)
                    last.then_inc(used, 1)

                def token_chunk(n, m, half):
                    slot = n % SPLIT_SLOTS
                    pe.wait_ge(lo_done, L * N_SPLIT + n + 1 + RAW_SLOTS)
                    b = 2 * m % 4
                    for kk in range(4):
                        k = 4 * half + kk
                        w = slice(kk * 512, (kk + 1) * 512)
                        for tt in range(TT):
                            tok = slice(tt * P, (tt + 1) * P)
                            dst = bank[b + tt][:, :]
                            nc.tensor.matmul(dst, h_hi[:, k, tok], w_hi[slot][:, w], start=(k == 0), stop=False)
                            nc.tensor.matmul(dst, h_lo[:, k, tok], w_hi[slot][:, w], start=False, stop=False)
                            last = nc.tensor.matmul(dst, h_hi[:, k, tok], w_lo[slot][:, w], start=False,
                                                    stop=(k == KD - 1))
                    last.then_inc(used, 1)

                def ada_rows(g, b):
                    for half in range(2):
                        r = RAW_OF[("ada", 2 * g + half)]
                        pe.wait_ge(raw_full[r % RAW_SLOTS], raw_need(L, r))
                        for kk in range(4):
                            last = nc.tensor.matmul(bank[b][32 * kk:32 * kk + 32, :], cond[:, 4 * half + kk, :],
                                                    raw[r % RAW_SLOTS][:, kk * 512:(kk + 1) * 512],
                                                    start=(half == 0), stop=(half == 1))
                        last.then_inc(ada_used, 1)

                def turn_rows(g):
                    pe.wait_ge(row_ev, L * ADA_GROUPS + g + 1)
                    for q in range(4):
                        rows = ada_rows_a[:, g, q * P:(q + 1) * P] if g < ADA_FIRST else ada_rows_b[:, q * P:(q + 1) * P]
                        dst = bank[6][:, 4 * g + q:4 * g + q + 1] if g < ADA_FIRST else bank[7][:, q:q + 1]
                        last = nc.tensor.matmul(dst, rows, ones[:, 0:1], start=True, stop=True)
                    last.then_inc(modt, 1)

                def sum_squares(i, src, tiles, b):
                    pe.wait_ge(sq_done, L * 3 + i + 1)
                    for tt in range(TT):
                        for c in range(tiles):
                            last = nc.tensor.matmul(bank[b][:, 256 + tt:257 + tt], src[:, c, tt * P:(tt + 1) * P],
                                                    ones[:, 0:1], start=(c == 0), stop=(c == tiles - 1))
                    last.then_inc(stat_mm, 1)

                def spread(i, b):
                    pe.wait_ge(diag_done, L * 3 + i + 1)
                    for tt in range(TT):
                        last = nc.tensor.matmul(bank[b][:, tt * P:(tt + 1) * P], ones[:, :], diag[:, tt, :],
                                                start=True, stop=True)
                    last.then_inc(bcast, 1)

                def transposes(src, sem_):
                    for b in range(2):
                        for a in range(2):
                            for tt in range(TT):
                                cc = 2 * b + a
                                last = nc.tensor.transpose(bank[4 + b][:, a * T + tt * P:a * T + (tt + 1) * P],
                                                           src[:, tt, cc * P:(cc + 1) * P], ident[:, :])
                        last.then_inc(sem_, 1)

                def attend(t):
                    if t < HEADS:
                        if t >= 1:
                            pe.wait_ge(s_ev, L * HEADS + t)
                        part = slice((t % 2) * HD, (t % 2 + 1) * HD)
                        qh, kh = qT[part, t // 2, :], kT[part, t // 2, :]
                        nc.tensor.matmul(bank[4][:, 0:P], qh[:, 0:P], kh[:, 0:P], start=True, stop=True)
                        nc.tensor.matmul(bank[4][:, P:3 * P], qh[:, P:T], kh[:, :], start=True,
                                         stop=True).then_inc(s_mm, 1)
                    if t >= 1:
                        if t >= 2:
                            pe.wait_ge(pt_ev, L * (HEADS + 1) + t - 1)
                            hh = t - 2
                            p_of = pT[:, hh % 2, :]
                            cols = slice(hh * HD, (hh + 1) * HD)
                            nc.tensor.matmul(bank[5][:, 3 * P:3 * P + HD], p_of[:, 0:P], v_tok[:, 0, cols],
                                             start=True, stop=True)
                            nc.tensor.matmul(bank[5][:, 3 * P + HD:4 * P], p_of[:, P:2 * P], v_tok[:, 0, cols],
                                             start=True, stop=False)
                            last = nc.tensor.matmul(bank[5][:, 3 * P + HD:4 * P], p_of[:, 2 * P:3 * P],
                                                    v_tok[:, 1, cols], start=False, stop=True)
                        if t <= HEADS:
                            pe.wait_ge(exp_done, L * HEADS + t)
                            for i in range(3):
                                last = nc.tensor.transpose(bank[5][:, i * P:(i + 1) * P],
                                                           probs[:, (t - 1) % 2, i * P:(i + 1) * P], ident[:, :])
                        last.then_inc(pt_mm, 1)

                for g in range(ADA_FIRST):
                    ada_rows(g, g)
                sum_squares(0, work, KD, 4)
                for g in range(ADA_FIRST):
                    turn_rows(g)
                spread(0, 4)

                for n in range(N_FFN):
                    if n < N_QKV:
                        def tile_ready(k):
                            pe.wait_ge(lo_h, L * 16 + k + 1)
                        chunk(n, [n], h_hi, h_lo, KD, tile_ready if n == 0 else None)
                    elif n < N_GATE:
                        m, half = divmod(n - N_QKV, 2)
                        if half == 0:
                            if m < 2:
                                pe.wait_ge(glu_done, L * 2 + m + 1)
                            else:
                                pe.wait_ge(qk_norm, L * 2 * TT + TT)
                        token_chunk(n, m, half)
                    elif n < N_PA:
                        j = n - N_GATE
                        if j < 2:
                            pe.wait_ge(qk_norm, L * 2 * TT + 2 * TT)
                        elif j < 4:
                            pe.wait_ge(v_ev, L * TT + TT)
                        else:
                            pe.wait_ge(gate_ev, L * 8 + j - 3)
                        chunk(n, [(2 + j) % 4], h_hi, h_lo, KD)
                    elif n < N_PB:
                        j = n - N_PA
                        pe.wait_ge(gate_ev, L * 8 + 6 + 2 * j)
                        pe.wait_ge(a_lo_done, L + 1)
                        chunk(n, [(2 + 2 * j) % 4, (3 + 2 * j) % 4], a_hi, a_lo, KC)
                    elif n < N_WO:
                        j = n - N_PB
                        pe.wait_ge(pa_ev, L * 4 + 2 + 2 * j)
                        pe.wait_ge(o_lo_done, L * 2 + 2)
                        chunk(n, [(2 + 2 * j) % 4, (3 + 2 * j) % 4], a_hi, a_lo, KC)
                    else:
                        j = n - N_WO
                        pe.wait_ge(pb_ev, L * 4 + (2 if j < 2 else 4))

                        def half_ready(k):
                            pe.wait_ge(m_lo_done, L * 2 + 1 + k // 4)
                        chunk(n, [(2 + j) % 4], h_hi, h_lo, KD, half_ready if j == 0 else None)

                    g = ada_group_after(n)
                    if g is not None:
                        pe.wait_ge(mod_done, L * ADA_GROUPS + g)
                        ada_rows(g, 7)
                    elif n >= 1 and ada_group_after(n - 1) is not None:
                        turn_rows(ADA_FIRST + (n - N_QKV) // 2)
                    if n == N_QKV + 3:
                        pe.wait_ge(qk_norm, L * 2 * TT + TT)
                        transposes(q_tok, qk_tr)
                    if n == N_QKV + 5:
                        pe.wait_ge(qk_norm, L * 2 * TT + 2 * TT)
                        pe.wait_ge(qk_ev, L * 4 + 2)
                        transposes(k_tok, qk_tr)
                    if n == N_GATE:
                        pe.wait_ge(qk_ev, L * 4 + 4)
                    if n == 16:
                        pe.wait_ge(conv, (L + 1) * len(CONV_OPS))
                        for t in range(KC):
                            last = nc.tensor.matmul(bank[6][:, 0:T], ones[:, :], acc[:, t, :], start=(t == 0),
                                                    stop=(t == KC - 1))
                        last.then_inc(mean_mm, 1)
                    if N_GATE <= n < N_GATE + HEADS + 2:
                        attend(n - N_GATE)
                    if n == 17:
                        sum_squares(1, lin, KC, 6)
                        spread(1, 6)
                    if n == N_PA + 1:
                        pe.wait_ge(pt_ev, L * (HEADS + 1) + HEADS + 1)
                        transposes(o_tok, o_tr)

                sum_squares(2, work, KD, 4)
                spread(2, 4)

                def up(n, b, first_k=None):
                    chunk(n, [b], h_hi, h_lo, KD, first_k)

                def up_ready(k):
                    pe.wait_ge(lo_h, L * 16 + 8 + k + 1)

                def down(n, i, parity):
                    slot = n_slot(n)
                    pe.wait_ge(lo_done, L * N_SPLIT + n + (1 + RAW_SLOTS))
                    pe.wait_ge(f_lo_done, L * PAIRS + i + 1)
                    for o in range(KD):
                        for kk in range(2):
                            col = kk * D + o * P
                            last = three(bank[4 + o // 2][:, (o % 2) * T:(o % 2 + 1) * T], w_lo[slot], w_hi[slot],
                                         slice(col, col + P), f_hi[:, parity, kk, :], f_lo[:, parity, kk, :],
                                         False, False, check=False)
                    last.then_inc(used, 1)

                def n_slot(n):
                    return slot_now[0]

                slot_now = [0]
                up(N_FFN, 0, up_ready)
                up(N_FFN + 1, 1)
                for b in range(4, 8):
                    nc.tensor.matmul(bank[b][:, :], zeros[:, 0:P], zeros[:, :], start=True, stop=True)

                with pe.Fori(0, (PAIRS - 1) // 2) as it:
                    for j in range(2):
                        i = it * 2 + (1 + j)
                        parity = (1 + j) % 2
                        base = N_FFN + 2 + 3 * j
                        for s in range(2):
                            slot = (base + s) % SPLIT_SLOTS
                            pe.wait_ge(lo_done, L * N_SPLIT + it * RAW_SLOTS + (base + s + 1 + RAW_SLOTS))
                            if s == 0:
                                pe.wait_ge(f_done, L * PAIRS + it * 2 + (j + 1))
                            for t in range(2):
                                for k in range(KD):
                                    col = k * 2 * P + t * P
                                    last = three(bank[2 * parity + s][:, t * T:(t + 1) * T], w_lo[slot], w_hi[slot],
                                                 slice(col, col + P), h_hi[:, k, :], h_lo[:, k, :],
                                                 k == 0, k == KD - 1)
                            last.then_inc(used, 1)
                        slot_now[0] = (base + 2) % SPLIT_SLOTS
                        down(it * RAW_SLOTS + (base + 2), it * 2 + j, (j) % 2)
                slot_now[0] = (N_SPLIT - 1) % SPLIT_SLOTS
                down(N_SPLIT - 1, PAIRS - 1, (PAIRS - 1) % 2)


def _stream(w):
    chunks = []

    def tall(m, rows, cols):
        b = m[rows, cols]
        return b.reshape(b.shape[0] // P, P, b.shape[1]).transpose(1, 0, 2).reshape(P, CH)

    every = slice(None)
    for l in range(DEPTH):
        w_in = w["w_in"][l]
        for kind, n in ORDER:
            if kind == "ada":
                g, half = divmod(n, 2)
                c = tall(w["ada_w"][l], slice(half * 512, half * 512 + 512), slice(g * 512, g * 512 + 512))
            elif n < N_QKV:
                j, gate = divmod(n, 2)
                at = gate * CONV_CH + j * 256
                c = tall(w_in, every, slice(at, at + 256))
            elif n < N_GATE:
                m, half = divmod(n - N_QKV, 2)
                at = 2 * CONV_CH + m * 512
                c = tall(w_in, slice(half * 512, half * 512 + 512), slice(at, at + 512))
            elif n < N_PA:
                at = 2 * CONV_CH + 3 * HEADS * HD + (n - N_GATE) * 256
                c = tall(w_in, every, slice(at, at + 256))
            elif n < N_WO:
                name = "w_pa" if n < N_PB else "w_pb"
                j = (n - N_PA) % 2
                c = tall(w[name][l], every, slice(j * 512, j * 512 + 512))
            elif n < N_FFN:
                at = (n - N_WO) * 256
                c = tall(w["w_o"][l], every, slice(at, at + 256))
            else:
                f = n - N_FFN
                if f < 2:
                    what, i = f, 0
                elif n == N_SPLIT - 1:
                    what, i = 2, PAIRS - 1
                else:
                    i, what = divmod(f - 2, 3)
                    i += what < 2
                if what < 2:
                    at = what * D_FF + i * 256
                    c = tall(w["w_up"][l], every, slice(at, at + 256))
                else:
                    c = tall(w["w_down"][l], slice(i * 256, i * 256 + 256), every)
            chunks.append(c)
    return np.stack(chunks)


def _packs(w):
    out = np.empty((P, DEPTH, NV), np.float32)

    def put(l, at, v):
        cols = v.reshape(-1, P).T
        out[:, l, at:at + cols.shape[1]] = cols

    for l in range(DEPTH):
        put(l, V_G1, w["norm1_g"][l])
        put(l, V_G2, w["norm2_g"][l])
        put(l, V_CW, w["conv_w"][l])
        put(l, V_CB, w["conv_b"][l])
        put(l, V_LG, w["conv_ln_g"][l])
        put(l, V_LB, w["conv_ln_b"][l])
        put(l, V_QG, np.concatenate([w["q_norm_g"][l]] * 2))
        put(l, V_KG, np.concatenate([w["k_norm_g"][l]] * 2))
        put(l, V_FW, w["ffn_conv_w"][l])
        put(l, V_FB, w["ffn_conv_b"][l])
        put(l, V_AB, w["ada_b"][l])
    return out


def _onehot():
    hot = np.zeros((BUCKETS + 1, TABLE), np.float32)
    exact = BUCKETS // 2
    for i in range(TABLE):
        dist = T - 1 - i
        if dist < 0:
            b = BUCKETS
        elif dist < exact:
            b = dist
        else:
            b = min(exact + int(math.log(dist / exact) / math.log(MAX_DISTANCE / exact) * (BUCKETS - exact)),
                    BUCKETS - 1)
        hot[b, i] = 1.0
    return hot


def kernel(**inputs):
    import concourse.bacc as bacc
    from concourse.bass_utils import run_bass_kernel_spmd

    w = {k: np.asarray(v) for k, v in inputs.items()}
    arrays = {
        "stream": _stream(w),
        "x": np.ascontiguousarray(w["x"][0].reshape(T, KD, P).transpose(2, 1, 0)),
        "c": np.ascontiguousarray(w["c"][0].reshape(KD, P).T),
        "packs": _packs(w),
        "rel": np.ascontiguousarray(w["rel_bias"].T),
        "onehot": _onehot(),
        "ident": np.eye(P, dtype=np.float32),
        "flip": np.ascontiguousarray(np.eye(P, dtype=np.float32)[::-1]),
    }
    nc = bacc.Bacc("TRN2", target_bir_lowering=False, num_devices=1)
    args = [nc.dram_tensor(f"in_{n}", a.shape, F32, kind="ExternalInput").ap() for n, a in arrays.items()]
    out = nc.dram_tensor("out_x", (P, KD, T), F32, kind="ExternalOutput").ap()
    trunk(nc, *args, out)
    r = run_bass_kernel_spmd(nc, [{f"in_{n}": a for n, a in arrays.items()}], core_ids=[0])
    got = r.results[0]["out_x"]
    return got.transpose(2, 1, 0).reshape(1, T, D)
```

```python
import math
from contextlib import ExitStack

import numpy as np

import concourse.bass as bass
from concourse import mybir

F32 = mybir.dt.float32
F32R = mybir.dt.float32r
BF16 = mybir.dt.bfloat16
ALU = mybir.AluOpType
ACT = mybir.ActivationFunctionType
AX = mybir.AxisListType

P = 128
D = 1024
T = 256
DEPTH = 2
CONV_CH = D // 2
TAPS = 31
HD = 64
HEADS = (D // 2) // HD
BUCKETS = 32
MAX_DISTANCE = 2048
D_FF = ((int(8 * D / 3) + 255) // 256) * 256
FTAPS = 3
EPS = 1e-6
KD = D // P
KC = CONV_CH // P
TT = T // P
PAIRS = D_FF // (2 * P)
KF = 2 * D_FF // P
CH = 2048
MASKED = -1.0e30

N_QKV = 0
N_CONV = 6
N_GATE = 10
N_PB = 18
N_PA = 20
N_WO = 22
N_FFN = 26
N_SPLIT = N_FFN + 3 * PAIRS
ADA_GROUPS = 6 * D // 512
ADA_FIRST = 4
ADA_LAST = 2
ADA_AFTER = 4
N_ADA = 2 * ADA_GROUPS
RAW_SLOTS = 6
SPLIT_SLOTS = 3
LOOKAHEAD = 2


def ada_group_after(n):
    g = ADA_FIRST + (n - ADA_AFTER) // 2
    if n >= ADA_AFTER and (n - ADA_AFTER) % 2 == 0 and g < ADA_GROUPS - ADA_LAST:
        return g
    return None


def stream_order():
    order = [("ada", a) for a in range(2 * ADA_FIRST)]
    for n in range(N_SPLIT):
        order.append(("split", n))
        g = ada_group_after(n)
        if g is not None:
            order += [("ada", 2 * g), ("ada", 2 * g + 1)]
        if n == N_FFN - 1:
            order += [("ada", a) for a in range(2 * (ADA_GROUPS - ADA_LAST), 2 * ADA_GROUPS)]
    return order


ORDER = stream_order()
N_RAW = len(ORDER)
RAW_OF = {what: r for r, what in enumerate(ORDER)}
FFN_ROUNDS = (PAIRS - 1) // 2
R_LOOP = RAW_OF[("split", N_FFN + 2)] + RAW_SLOTS
USES = [sum(r % RAW_SLOTS == s for r in range(N_RAW)) for s in range(RAW_SLOTS)]

V_G1 = 0
V_G2 = V_G1 + KD
V_CW = V_G2 + KD
V_CB = V_CW + TAPS * KC
V_LG = V_CB + KC
V_LB = V_LG + KC
V_QG = V_LB + KC
V_KG = V_QG + 1
V_FW = V_KG + 1
V_FB = V_FW + FTAPS * KF
V_AB = V_FB + KF
NV = V_AB + 6 * KD
M_SH1, M_SC1, M_GA1, M_SH2, M_SC2, M_GA2 = (KD * i for i in range(6))

TABLE = 2 * T - P - 1
CONV_OPS = [(tap, t) for half in (0, 2) for tap in range(TAPS) for t in (half, half + 1)]
CONV_FROM = 8
CONV_SHARES = [11, 11, 11, 11, 11, 11, 11, 15, 16, 16]
N_ATTEND = 6
CONV_BANKS = (2, 3, 0, 1)


def conv_share(n):
    at = n - CONV_FROM
    if not 0 <= at < len(CONV_SHARES):
        return []
    return range(sum(CONV_SHARES[:at]), sum(CONV_SHARES[:at + 1]))


assert sum(CONV_SHARES) == len(CONV_OPS)


def trunk(nc, stream, x_in, c_in, packs_in, rel_in, onehot_in, ident_in, flip_in, out):
    ctx = ExitStack()
    with ctx:
        def sb(name, shape, dt=F32):
            return ctx.enter_context(nc.sbuf_tensor(name, shape, dt))

        def sem(name):
            return ctx.enter_context(nc.semaphore(name))

        raw = [sb(f"raw{i}", [P, CH]) for i in range(RAW_SLOTS)]
        w_hi = [sb(f"w_hi{i}", [P, CH], F32R) for i in range(SPLIT_SLOTS)]
        w_lo = [sb(f"w_lo{i}", [P, CH], F32R) for i in range(SPLIT_SLOTS)]
        x = sb("x", [P, KD, T])
        h_hi = sb("h_hi", [P, KD, T], F32R)
        h_lo = sb("h_lo", [P, KD, T], F32R)
        work = sb("work", [P, KD, T])
        q_tok = work[:, 0:4, :].rearrange("p (a b) t -> p a (b t)", a=TT)
        k_tok = work[:, 4:8, :].rearrange("p (a b) t -> p a (b t)", a=TT)
        gates = sb("gates", [P, 2 * KD, T])
        ada_rows_a = gates[:, 0:8, :].rearrange("p (a b) t -> p a (b t)", a=ADA_FIRST)
        ada_rows_b = sb("ada_rows_b", [P, 512])
        glu = sb("glu", [P, KC, TAPS - 1 + T])
        acc = sb("acc", [P, KC, T])
        lin = sb("lin", [P, KC, T])
        a_hi = sb("a_hi", [P, KC, T], F32R)
        a_lo = sb("a_lo", [P, KC, T], F32R)
        o_hi = sb("o_hi", [P, KC, T], F32R)
        o_lo = sb("o_lo", [P, KC, T], F32R)
        v_tok = sb("v_tok", [P, TT, 512])
        ada_rows_c = lin[:, 0:2, :].rearrange("p a t -> p (a t)")
        qT = sb("qT", [P, KC, T])
        kT = sb("kT", [P, KC, T])
        bias = sb("bias", [P, HEADS, T])
        probs = k_tok[:, :, 0:3 * P]
        pT = sb("pT", [P, 2, 3 * P])
        o_tok = q_tok
        u = gates[:, 0:4, :]
        f_hi = a_hi[:, :, :].rearrange("p (a b) t -> p a b t", a=2)
        f_lo = a_lo[:, :, :].rearrange("p (a b) t -> p a b t", a=2)
        packs = sb("packs", [P, DEPTH, NV])
        vec = sb("vec", [P, NV])
        mod = sb("mod", [P, 6 * KD])
        gs = sb("gs", [P, 2, KD])
        qg8 = sb("qg8", [P, 1])
        cT = sb("cT", [P, KD])
        cond = sb("cond", [P, KD, 32])
        ident = sb("ident", [P, P])
        ones = sb("ones", [P, P])
        zeros = sb("zeros", [P, 512], BF16)
        neg_half = sb("neg_half", [P, 16])
        stat = sb("stat", [P, TT])
        rstd = sb("rstd", [P, TT])
        diag = sb("diag", [P, TT, P])
        qk_stat = sb("qk_stat", [P, 2, TT * HEADS])
        qk_rstd = sb("qk_rstd", [P, 2, TT * HEADS])
        row_max = sb("row_max", [P, HEADS, TT])
        row_sum = sb("row_sum", [P, HEADS, TT])
        row_inv = sb("row_inv", [P, HEADS, TT])
        rel = sb("rel", [BUCKETS + 1, HEADS])
        onehot = gates[0:BUCKETS + 1, 8:10, :].rearrange("p a t -> p (a t)")[:, 0:TABLE]
        table = gates[0:HEADS, 10:12, :].rearrange("p a t -> p (a t)")[:, 0:TABLE]
        flip = gates[:, 12, 0:P]
        table_dram = nc.dram_tensor("table_scratch", (HEADS, TABLE), F32, kind="Internal").ap()

        bank = [ctx.enter_context(nc.psum_tensor(f"bank{i}", [P, 512], F32)) for i in range(8)]

        raw_full = [sem(f"raw_full{i}") for i in range(RAW_SLOTS)]
        hi_done = sem("hi_done")
        lo_done = sem("lo_done")
        used = sem("used")
        ada_used = sem("ada_used")
        row_ev = sem("row_ev")
        modt = sem("modt")
        mod_done = sem("mod_done")
        vec_done = sem("vec_done")
        gs_done = sem("gs_done")
        sq_x = sem("sq_x")
        sq_ln = sem("sq_ln")
        stat_mm = sem("stat_mm")
        stat_ev = sem("stat_ev")
        rstd_done = sem("rstd_done")
        diag_done = sem("diag_done")
        bcast = sem("bcast")
        xn_done = sem("xn_done")
        hi_h = sem("hi_h")
        aff_h = sem("aff_h")
        lo_h = sem("lo_h")
        bank_mm = sem("bank_mm")
        cg_sig = sem("cg_sig")
        glu_done = sem("glu_done")
        conv = sem("conv")
        mean_mm = sem("mean_mm")
        cen_done = sem("cen_done")
        cn_done = sem("cn_done")
        ln_sig = sem("ln_sig")
        ln_aff = sem("ln_aff")
        a_done = sem("a_done")
        a_hi_done = sem("a_hi_done")
        a_lo_done = sem("a_lo_done")
        qk_sq = sem("qk_sq")
        qk_red = sem("qk_red")
        qk_mean = sem("qk_mean")
        qk_pow = sem("qk_pow")
        qk_norm = sem("qk_norm")
        qk_tr = sem("qk_tr")
        qk_ev = sem("qk_ev")
        v_ev = sem("v_ev")
        gate_ev = sem("gate_ev")
        gate_sig = sem("gate_sig")
        s_mm = sem("s_mm")
        s_ev = sem("s_ev")
        max_done = sem("max_done")
        max_raw = sem("max_raw")
        exp_done = sem("exp_done")
        inv_done = sem("inv_done")
        pt_mm = sem("pt_mm")
        pt_ev = sem("pt_ev")
        o_tr = sem("o_tr")
        o_hi_done = sem("o_hi_done")
        o_lo_done = sem("o_lo_done")
        pa_ev = sem("pa_ev")
        pb_ev = sem("pb_ev")
        m_done = sem("m_done")
        m_hi_done = sem("m_hi_done")
        m_lo_done = sem("m_lo_done")
        x_upd = sem("x_upd")
        u_ev = sem("u_ev")
        u_conv = sem("u_conv")
        u_silu = sem("u_silu")
        f_done = sem("f_done")
        f_hi_done = sem("f_hi_done")
        f_lo_done = sem("f_lo_done")
        ld_small = [sem(f"ld_small{i}") for i in range(7)]
        const_done = sem("const_done")
        cond_done = sem("cond_done")
        rel_done = sem("rel_done")
        table_mm = sem("table_mm")
        table_ev = sem("table_ev")
        table_out = sem("table_out")
        bias_in = sem("bias_in")
        bias_mm = sem("bias_mm")
        bias_done = sem("bias_done")
        bias_asked = sem("bias_asked")
        stored = sem("stored")

        def raw_need(L, r, uses_more=0):
            return L * (16 * USES[r % RAW_SLOTS]) + (16 * (r // RAW_SLOTS + 1) + 16 * uses_more)

        def wo_place(j, t):
            if (j, t) == (3, 1):
                return 5, slice(0, T)
            return (2 + j) % 4, slice(t * T, (t + 1) * T)

        block = ctx.enter_context(nc.Block())

        @block.sync
        def _(sp):
            def fetch(r_of_all, slot):
                sp.dma_start(raw[slot][:, :], stream[r_of_all, :, :]).then_inc(raw_full[slot], 16)

            def load(L, r):
                before = r - RAW_SLOTS
                lower = 0
                if before < 0:
                    before = max(q for q in range(N_RAW) if q % RAW_SLOTS == r % RAW_SLOTS)
                    lower = N_SPLIT
                kind, n = ORDER[before]
                if kind == "split":
                    sp.wait_ge(lo_done, L * N_SPLIT + (n + 1 - lower + RAW_SLOTS))
                else:
                    sp.wait_ge(ada_used, L * N_ADA + (n + 1))
                fetch(L * N_RAW + r, r % RAW_SLOTS)

            sp.dma_start(x[:, :, :], x_in).then_inc(ld_small[0], 16)
            sp.dma_start(cT[:, :], c_in).then_inc(ld_small[1], 16)
            sp.dma_start(packs[:, :, :], packs_in).then_inc(ld_small[2], 16)
            with sp.Fori(0, DEPTH) as L:
                for r in range(R_LOOP):
                    if r == 2:
                        sp.wait_ge(bias_asked, 1)
                    load(L, r)
                with sp.Fori(0, FFN_ROUNDS - 1) as it:
                    for j in range(RAW_SLOTS):
                        sp.wait_ge(lo_done, L * N_SPLIT + it * RAW_SLOTS
                                   + (ORDER[R_LOOP + j - RAW_SLOTS][1] + 1 + RAW_SLOTS))
                        fetch(L * N_RAW + it * RAW_SLOTS + (R_LOOP + j), (R_LOOP + j) % RAW_SLOTS)
                load(L, N_RAW - 1)
            sp.wait_ge(x_upd, (2 * DEPTH + 1) * KD)
            sp.dma_start(out, x[:, :, :]).then_inc(stored, 16)
            sp.wait_ge(stored, 16)

        @block.gpsimd
        def _(pool):
            nc.gpsimd.memset(ones[:, :], 1.0)
            nc.gpsimd.memset(neg_half[:, :], -0.5)
            nc.gpsimd.memset(zeros[:, :], 0.0)
            nc.gpsimd.memset(glu[:, :, 0:TAPS - 1], 0.0)
            nc.gpsimd.memset(cond[:, :, :], 0.0).then_inc(const_done, 1)
            pool.wait_ge(ld_small[2], 16)
            with pool.Fori(0, DEPTH) as L:
                pool.wait_ge(x_upd, L * (2 * KD) + KD)
                nc.gpsimd.tensor_copy(vec[:, :], packs[:, L, :]).then_inc(vec_done, 1)

                def power(i):
                    pool.wait_ge(stat_ev, L * 3 + (i + 1))
                    nc.gpsimd.tensor_tensor(rstd[:, :], stat[:, :], neg_half[:, 0:TT],
                                            ALU.pow).then_inc(rstd_done, 1)

                power(0)
                for m in range(2):
                    pool.wait_ge(qk_mean, L * 2 + (m + 1))
                    nc.gpsimd.tensor_tensor(qk_rstd[:, m, :], qk_stat[:, m, :], neg_half[:, :],
                                            ALU.pow).then_inc(qk_pow, 1)
                power(1)
                power(2)

        @block.scalar
        def _(act):
            act.dma_start(ident[:, :], ident_in).then_inc(ld_small[3], 16)
            act.dma_start(rel[0:BUCKETS, :], rel_in).then_inc(ld_small[4], 16)
            act.dma_start(onehot[:, :], onehot_in).then_inc(ld_small[5], 16)
            act.dma_start(flip[:, :], flip_in).then_inc(ld_small[6], 16)
            act.wait_ge(ld_small[1], 16)
            act.wait_ge(const_done, 1)
            nc.scalar.activation(cond[:, :, 0], cT[:, :], ACT.Silu).then_inc(cond_done, 1)
            act.wait_ge(table_ev, 1)
            act.dma_start(table_dram, table[:, :]).then_inc(table_out, 16)
            act.wait_ge(table_out, 16)
            for i, part in enumerate((acc, lin)):
                src = bass.AP(tensor=table_dram.tensor, offset=4 * i * TABLE, ap=[[1, P], [TABLE, 4], [1, T]])
                act.dma_start(part[:, :, :], src).then_inc(bias_in, 16)
            act.sem_inc(bias_asked, 1)
            act.wait_ge(ld_small[0], 16)
            with act.Fori(0, DEPTH) as L:
                def split(n, it=0):
                    slot = n % SPLIT_SLOTS
                    r = RAW_OF[("split", n)]
                    act.wait_ge(raw_full[r % RAW_SLOTS], raw_need(L, r, it))
                    if n >= SPLIT_SLOTS:
                        act.wait_ge(used, L * N_SPLIT + it * RAW_SLOTS + (n + 1 - SPLIT_SLOTS))
                    else:
                        act.wait_ge(vec_done, L + 1)
                    nc.scalar.activation(w_hi[slot][:, :], raw[r % RAW_SLOTS][:, :],
                                         ACT.Copy).then_inc(hi_done, 1)

                def rows(g):
                    act.wait_ge(ada_used, L * N_ADA + 2 * (g + 1))
                    if g < ADA_FIRST:
                        dst, src = ada_rows_a[:, g, :], bank[g]
                    elif g < ADA_GROUPS - 1:
                        act.wait_ge(modt, L * ADA_GROUPS + g)
                        dst, src = ada_rows_b[:, :], bank[7]
                    else:
                        dst, src = ada_rows_c, bank[6]
                    nc.scalar.activation(dst, src[:, :], ACT.Copy).then_inc(row_ev, 1)

                def squares(i):
                    for c in range(0, KD, 2):
                        act.wait_ge(x_upd, L * (2 * KD) + (i * KD + c + 2))
                        if i == 0 and c == 0:
                            act.wait_ge(vec_done, L + 1)
                        nc.scalar.activation(work[:, c:c + 2, :], x[:, c:c + 2, :],
                                             ACT.Square).then_inc(sq_x, 1)

                def high_h(i):
                    act.wait_ge(gs_done, L * 3 + (1 if i == 0 else 3))
                    for c in range(KD):
                        act.wait_ge(xn_done, L * 8 + i * 4 + c // 2 + 1)
                        shift = (M_SH1 if i == 0 else M_SH2) + c
                        nc.scalar.activation(h_hi[:, c, :], work[:, c, :], ACT.Identity,
                                             bias=mod[:, shift:shift + 1],
                                             scale=gs[:, i, c:c + 1]).then_inc(hi_h, 1)

                squares(0)
                for g in range(ADA_FIRST):
                    rows(g)
                split(0)
                high_h(0)
                split(1)

                def conv_gate(j):
                    act.wait_ge(used, L * N_SPLIT + N_CONV + 2 * j + 2)
                    if j == 0:
                        act.wait_ge(modt, L * ADA_GROUPS + ADA_FIRST)
                    nc.scalar.activation(gates[:, 2 * j:2 * j + 2, :],
                                         bank[CONV_BANKS[2 * j + 1]][:, :].rearrange("p (a t) -> p a t", a=2),
                                         ACT.Sigmoid).then_inc(cg_sig, 1)

                def qk_squares(m):
                    act.wait_ge(used, L * N_SPLIT + N_QKV + 2 * m + 2)
                    for tt in range(TT):
                        if m == 1:
                            act.wait_ge(qk_red, L * 2 * TT + tt + 1)
                        nc.scalar.activation(lin[:, 2 * tt:2 * tt + 2, :],
                                             bank[2 * m + tt][:, :].rearrange("p (a t) -> p a t", a=2),
                                             ACT.Square).then_inc(qk_sq, 1)

                def qk_copy(m):
                    if m == 0:
                        act.wait_ge(gs_done, L * 3 + 2)
                    for b in range(2):
                        act.wait_ge(qk_tr, L * 4 + 2 * m + b + 1)
                        dst = (qT if m == 0 else kT)[:, 2 * b:2 * b + 2, :]
                        gain = qg8[:, 0:1] if m == 0 else vec[:, V_KG:V_KG + 1]
                        nc.scalar.activation(dst, bank[4 + b][:, :].rearrange("p (a t) -> p a t", a=2),
                                             ACT.Copy, scale=gain).then_inc(qk_ev, 1)

                def v_copy():
                    act.wait_ge(used, L * N_SPLIT + N_QKV + 6)
                    for tt in range(TT):
                        nc.scalar.activation(v_tok[:, tt, :], bank[tt][:, :], ACT.Copy).then_inc(v_ev, 1)

                def gate_copy(j, func):
                    act.wait_ge(used, L * N_SPLIT + N_GATE + j + 1)
                    if j < 2:
                        act.wait_ge(glu_done, L * 2 + 2)
                    nc.scalar.activation(gates[:, 2 * j:2 * j + 2, :],
                                         bank[(2 + j) % 4][:, :].rearrange("p (a t) -> p a t", a=2),
                                         func).then_inc(gate_ev, 1)

                def exponentials(t):
                    act.wait_ge(max_done, L * HEADS + t + 1)
                    nc.scalar.activation(probs[:, t % 2, 0:P], probs[:, t % 2, 0:P], ACT.Exp,
                                         bias=row_max[:, t, 0:1], accum_out=row_sum[:, t, 0:1])
                    nc.scalar.activation(probs[:, t % 2, P:3 * P], probs[:, t % 2, P:3 * P], ACT.Exp,
                                         bias=row_max[:, t, 1:2],
                                         accum_out=row_sum[:, t, 1:2]).then_inc(exp_done, 1)

                def attend(t):
                    act.wait_ge(pt_mm, L * (HEADS + 1) + t)
                    if t >= 2:
                        hh = t - 2
                        act.wait_ge(inv_done, L * HEADS + hh + 1)
                        for tt in range(TT):
                            last = nc.scalar.activation(
                                o_tok[:, tt, hh * HD:(hh + 1) * HD],
                                bank[5][:, 3 * P + tt * HD:3 * P + (tt + 1) * HD],
                                ACT.Copy, scale=row_inv[:, hh, tt:tt + 1])
                    if t <= HEADS:
                        last = nc.scalar.activation(pT[:, (t - 1) % 2, :], bank[5][:, 0:3 * P], ACT.Copy)
                    last.then_inc(pt_ev, 1)

                def ln_squares():
                    act.wait_ge(cen_done, L + 1)
                    nc.scalar.activation(lin[:, :, :], acc[:, :, :], ACT.Square).then_inc(sq_ln, 1)

                def ln_tail():
                    act.wait_ge(cn_done, L + 1)
                    for t in range(KC):
                        nc.scalar.activation(lin[:, t, :], acc[:, t, :], ACT.Sigmoid,
                                             bias=vec[:, V_LB + t:V_LB + t + 1],
                                             scale=vec[:, V_LG + t:V_LG + t + 1]).then_inc(ln_sig, 1)
                    for t in range(KC):
                        act.wait_ge(a_done, L * KC + t + 1)
                        nc.scalar.activation(a_hi[:, t, :], acc[:, t, :], ACT.Copy).then_inc(a_hi_done, 1)

                def gate_sigmoids():
                    for part in (gates[:, 0:KD, :], gates[:, KD:KD + 2, :]):
                        nc.scalar.activation(part, part, ACT.Sigmoid).then_inc(gate_sig, 1)

                def o_high():
                    for b in range(2):
                        act.wait_ge(o_tr, L * 2 + b + 1)
                        nc.scalar.activation(o_hi[:, 2 * b:2 * b + 2, :],
                                             bank[4 + b][:, :].rearrange("p (a t) -> p a t", a=2),
                                             ACT.Copy).then_inc(o_hi_done, 1)

                def m_high(i):
                    act.wait_ge(m_done, L * 4 + i + 1)
                    nc.scalar.activation(h_hi[:, 2 * i:2 * i + 2, :], gates[:, 2 * i:2 * i + 2, :],
                                         ACT.Copy).then_inc(m_hi_done, 1)

                for n in range(N_FFN):
                    turn = n - N_ATTEND
                    if n == 18:
                        ln_squares()
                    split(n + LOOKAHEAD)
                    if n == 4:
                        qk_copy(0)
                    if n == 6:
                        qk_copy(1)
                    if n == 16:
                        gate_sigmoids()
                    if n == 17:
                        o_high()
                    if n == 19:
                        ln_tail()
                    if 0 <= turn - 1 < HEADS:
                        exponentials(turn - 1)
                    if n in (1, 3):
                        qk_squares(n // 2)
                    if n == 5:
                        v_copy()
                    if n in (N_CONV + 1, N_CONV + 3):
                        conv_gate((n - N_CONV) // 2)
                    if N_GATE <= n < N_PB:
                        gate_copy(n - N_GATE, ACT.Copy if n < 15 else ACT.Sigmoid)
                    g = ada_group_after(n)
                    if g is not None:
                        rows(g)
                    if 1 <= turn <= HEADS + 1:
                        attend(turn)
                    if N_PA <= n < N_WO:
                        m_high(2 * (n - N_PA))
                        m_high(2 * (n - N_PA) + 1)
                squares(1)
                rows(ADA_GROUPS - 2)
                split(N_FFN + 2)
                rows(ADA_GROUPS - 1)
                high_h(1)
                split(N_FFN + 3)

                def ffn(i, first, parity, opening=False):
                    for s in range(2):
                        act.wait_ge(used, L * N_SPLIT + (first + s + 1))
                        if s == 0 and not opening:
                            act.wait_ge(f_lo_done, L * PAIRS + i)
                        for t in range(2):
                            col = 2 * i + t + s * (KF // 2)
                            b = bank[2 * parity + s]
                            nc.scalar.activation(u[:, 2 * s + t, :], b[:, t * T:(t + 1) * T], ACT.Identity,
                                                 bias=at(V_FB, col), scale=at(V_FW + 2 * KF, col)).then_inc(u_ev, 1)
                    act.wait_ge(u_conv, L * 8 * PAIRS + i * 8 + 8)
                    nc.scalar.activation(u[:, 2:4, :], u[:, 2:4, :], ACT.Silu).then_inc(u_silu, 1)
                    act.wait_ge(f_done, L * PAIRS + i + 2)
                    nc.scalar.activation(f_hi[:, parity, :, :], u[:, 0:2, :], ACT.Copy).then_inc(f_hi_done, 1)

                def at(base, col):
                    if isinstance(col, int):
                        return vec[:, base + col:base + col + 1]
                    return vec[:, bass.ds(col + base, 1)]

                ffn(0, N_FFN, 0, opening=True)

                def ffn_round(it, last):
                    for j in range(2):
                        base = N_FFN + 2 + 3 * j
                        split(base + 2, it=it)
                        if last and j == 1:
                            split(base + 3, it=it)
                        else:
                            split(base + 3, it=it)
                            split(base + 4, it=it)
                        i = it * 2 + (1 + j)
                        ffn(i, it * RAW_SLOTS + base, (1 + j) % 2)

                with act.Fori(0, (PAIRS - 1) // 2 - 1) as it:
                    ffn_round(it, False)
                ffn_round((PAIRS - 1) // 2 - 1, True)

        @block.vector
        def _(dve):
            dve.sem_inc(lo_done, RAW_SLOTS)
            dve.sem_inc(f_done, 1)
            dve.wait_ge(ld_small[4], 16)
            nc.vector.memset(rel[BUCKETS:BUCKETS + 1, :], MASKED).then_inc(rel_done, 1)
            dve.wait_ge(table_mm, 1)
            nc.vector.tensor_copy(table[:, :], bank[0][0:HEADS, 0:TABLE]).then_inc(table_ev, 1)
            dve.wait_ge(bias_mm, 1)
            for i in range(4):
                last = nc.vector.tensor_copy(bias[:, 2 * i:2 * i + 2, :],
                                             bank[i][:, :].rearrange("p (a t) -> p a t", a=2))
            last.then_inc(bias_done, 1)
            dve.wait_ge(ld_small[0], 16)
            dve.sem_inc(x_upd, KD)
            dve.wait_ge(ld_small[3], 16)
            with dve.Fori(0, DEPTH) as L:
                def split(n, it=0):
                    slot = n % SPLIT_SLOTS
                    r = RAW_OF[("split", n)]
                    dve.wait_ge(hi_done, L * N_SPLIT + it * RAW_SLOTS + n + 1)
                    nc.vector.tensor_tensor(w_lo[slot][:, :], raw[r % RAW_SLOTS][:, :],
                                            w_hi[slot][:, :].bitcast(F32), ALU.subtract).then_inc(lo_done, 1)

                def mean_square(i, width, b):
                    dve.wait_ge(stat_mm, L * 3 + i + 1)
                    nc.vector.tensor_scalar(stat[:, :], bank[b][:, 256:256 + TT], 1.0 / width, EPS,
                                            ALU.mult, ALU.add).then_inc(stat_ev, 1)

                def diagonal(i):
                    dve.wait_ge(rstd_done, L * 3 + i + 1)
                    for tt in range(TT):
                        last = nc.vector.tensor_scalar(diag[:, tt, :], ident[:, :], rstd[:, tt:tt + 1], None,
                                                       ALU.mult)
                    last.then_inc(diag_done, 1)

                def scale_x(i):
                    dve.wait_ge(bcast, L * 3 + (1 if i == 0 else 3))
                    for c in range(0, KD, 2):
                        nc.vector.tensor_tensor(work[:, c:c + 2, :], x[:, c:c + 2, :],
                                                bank[4][:, 0:T].unsqueeze(1).broadcast_to((P, 2, T)),
                                                ALU.mult).then_inc(xn_done, 1)

                def norm_gain(i):
                    sc = M_SC1 if i == 0 else M_SC2
                    g = V_G1 if i == 0 else V_G2
                    nc.vector.scalar_tensor_tensor(gs[:, i, :], mod[:, sc:sc + KD], 1.0, vec[:, g:g + KD],
                                                   op0=ALU.add, op1=ALU.mult).then_inc(gs_done, 1)

                def low_h(i):
                    shift = M_SH1 if i == 0 else M_SH2
                    for c in range(KD + 1):
                        if c < KD:
                            dve.wait_ge(hi_h, L * 16 + i * 8 + c + 1)
                            nc.vector.tensor_scalar(work[:, c, :], work[:, c, :], gs[:, i, c:c + 1],
                                                    mod[:, shift + c:shift + c + 1],
                                                    ALU.mult, ALU.add).then_inc(aff_h, 1)
                        if c >= 1:
                            dve.wait_ge(aff_h, L * 16 + i * 8 + c)
                            nc.vector.tensor_tensor(h_lo[:, c - 1, :], work[:, c - 1, :],
                                                    h_hi[:, c - 1, :].bitcast(F32),
                                                    ALU.subtract).then_inc(lo_h, 1)

                def mod_columns(g, count, src):
                    dve.wait_ge(modt, L * ADA_GROUPS + g + count)
                    cols = slice(4 * g, 4 * (g + count))
                    ada_b = vec[:, V_AB + cols.start:V_AB + cols.stop]
                    nc.vector.tensor_tensor(mod[:, cols], src, ada_b, ALU.add).then_inc(mod_done, count)

                mean_square(0, D, 4)
                diagonal(0)
                scale_x(0)
                dve.wait_ge(vec_done, L + 1)
                mod_columns(0, ADA_FIRST, bank[6][:, 0:4 * ADA_FIRST])
                dve.wait_ge(mod_done, L * ADA_GROUPS + ADA_FIRST)
                norm_gain(0)
                nc.vector.tensor_scalar(qg8[:, :], vec[:, V_QG:V_QG + 1], HD ** -0.5, None,
                                        ALU.mult).then_inc(gs_done, 1)
                split(0)
                low_h(0)
                split(1)

                def glu_half(j):
                    dve.wait_ge(cg_sig, L * 2 + j + 1)
                    nc.vector.tensor_tensor(glu[:, 2 * j:2 * j + 2, TAPS - 1:],
                                            bank[CONV_BANKS[2 * j]][:, :].rearrange("p (a t) -> p a t", a=2),
                                            gates[:, 2 * j:2 * j + 2, :], ALU.mult).then_inc(glu_done, 1)

                def conv_steps(n):
                    for i in conv_share(n):
                        tap, t = CONV_OPS[i]
                        w = vec[:, V_CW + tap * KC + t:V_CW + tap * KC + t + 1]
                        src = glu[:, t, tap:tap + T]
                        if tap == 0:
                            dve.wait_ge(glu_done, L * 2 + t // 2 + 1)
                            nc.vector.tensor_scalar(acc[:, t, :], src, w, vec[:, V_CB + t:V_CB + t + 1],
                                                    ALU.mult, ALU.add).then_inc(conv, 1)
                        else:
                            dve.wait_ge(conv, L * len(CONV_OPS) + i - 1)
                            nc.vector.scalar_tensor_tensor(acc[:, t, :], src, w, acc[:, t, :],
                                                           op0=ALU.mult, op1=ALU.add).then_inc(conv, 1)

                def qk_sums(m):
                    for tt in range(TT):
                        dve.wait_ge(qk_sq, L * 2 * TT + m * TT + tt + 1)
                        nc.vector.reduce_sum(qk_stat[:, m, tt * HEADS:(tt + 1) * HEADS],
                                             lin[:, 2 * tt:2 * tt + 2, :].rearrange("p a (h d) -> p (a h) d", d=HD),
                                             AX.X).then_inc(qk_red, 1)
                    dve.wait_ge(qk_red, L * 2 * TT + (m + 1) * TT)
                    nc.vector.tensor_scalar(qk_stat[:, m, :], qk_stat[:, m, :], 1.0 / HD, EPS,
                                            ALU.mult, ALU.add).then_inc(qk_mean, 1)

                def qk_scale(m):
                    dve.wait_ge(qk_pow, L * 2 + m + 1)
                    for tt in range(TT):
                        dst = (q_tok if m == 0 else k_tok)[:, tt, :]
                        r = qk_rstd[:, m, tt * HEADS:(tt + 1) * HEADS]
                        nc.vector.tensor_tensor(dst.rearrange("p (h d) -> p h d", d=HD),
                                                bank[2 * m + tt][:, :].rearrange("p (h d) -> p h d", d=HD),
                                                r.unsqueeze(2).broadcast_to((P, HEADS, HD)),
                                                ALU.mult).then_inc(qk_norm, 1)

                def scores(t):
                    dve.wait_ge(s_mm, L * HEADS + t + 1)
                    if t >= 2:
                        dve.wait_ge(pt_mm, L * (HEADS + 1) + t - 1)
                    nc.vector.tensor_tensor(probs[:, t % 2, 0:P], bank[4][:, 0:P], bias[:, t, P:2 * P], ALU.add)
                    nc.vector.tensor_tensor(probs[:, t % 2, P:3 * P], bank[4][:, P:3 * P], bias[:, t, :],
                                            ALU.add).then_inc(s_ev, 1)
                    dve.wait_ge(s_ev, L * HEADS + t + 1)
                    nc.vector.reduce_max(row_max[:, t, 0:1], probs[:, t % 2, 0:P], AX.X)
                    nc.vector.reduce_max(row_max[:, t, 1:2], probs[:, t % 2, P:3 * P], AX.X).then_inc(max_raw, 1)
                    dve.wait_ge(max_raw, L * HEADS + t + 1)
                    nc.vector.tensor_scalar(row_max[:, t, :], row_max[:, t, :], -1.0, None,
                                            ALU.mult).then_inc(max_done, 1)

                def inverse(t):
                    dve.wait_ge(exp_done, L * HEADS + t + 1)
                    nc.vector.reciprocal(row_inv[:, t, :], row_sum[:, t, :]).then_inc(inv_done, 1)

                def centre():
                    dve.wait_ge(mean_mm, L + 1)
                    nc.vector.scalar_tensor_tensor(
                        acc[:, :, :], bank[6][:, 0:T].unsqueeze(1).broadcast_to((P, KC, T)),
                        -1.0 / CONV_CH, acc[:, :, :], op0=ALU.mult, op1=ALU.add).then_inc(cen_done, 1)

                def ln_tail():
                    dve.wait_ge(bcast, L * 3 + 2)
                    nc.vector.tensor_tensor(acc[:, :, :], acc[:, :, :],
                                            bank[6][:, 0:T].unsqueeze(1).broadcast_to((P, KC, T)),
                                            ALU.mult).then_inc(cn_done, 1)

                def ln_silu():
                    for t in range(KC):
                        dve.wait_ge(ln_sig, L * KC + t + 1)
                        nc.vector.tensor_scalar(acc[:, t, :], acc[:, t, :], vec[:, V_LG + t:V_LG + t + 1],
                                                vec[:, V_LB + t:V_LB + t + 1],
                                                ALU.mult, ALU.add).then_inc(ln_aff, 1)
                        if t >= 1:
                            silu_tile(t - 1)
                    silu_tile(KC - 1)
                    for t in range(KC):
                        dve.wait_ge(a_hi_done, L * KC + t + 1)
                        nc.vector.tensor_tensor(a_lo[:, t, :], acc[:, t, :], a_hi[:, t, :].bitcast(F32),
                                                ALU.subtract).then_inc(a_lo_done, 1)

                def silu_tile(t):
                    dve.wait_ge(ln_aff, L * KC + t + 1)
                    nc.vector.tensor_tensor(acc[:, t, :], acc[:, t, :], lin[:, t, :], ALU.mult).then_inc(a_done, 1)

                def merge_b(j):
                    if j == 0:
                        dve.wait_ge(gate_sig, L * 2 + 2)
                        dve.wait_ge(gate_ev, L * 8 + 8)
                    for b in range(2):
                        ready(N_PB + j, 2 * b + 1, j)
                        g = gates[:, KD + 4 * j + 2 * b:KD + 4 * j + 2 * b + 2, :]
                        nc.vector.tensor_tensor(g, bank[(2 + 2 * j + b) % 4][:, :].rearrange("p (a t) -> p a t", a=2),
                                                g, ALU.mult).then_inc(pb_ev, 1)

                def ready(n, tiles, early):
                    if tiles == 1:
                        dve.wait_ge(bank_mm, L * 8 + early + 1)
                    else:
                        dve.wait_ge(used, L * N_SPLIT + n + 1)

                def merge_a(j):
                    for b in range(2):
                        ready(N_PA + j, 2 * b + 1, 2 + j)
                        i = 2 * j + b
                        g, other = gates[:, 2 * i:2 * i + 2, :], gates[:, KD + 2 * i:KD + 2 * i + 2, :]
                        nc.vector.tensor_tensor(g, bank[(2 + i) % 4][:, :].rearrange("p (a t) -> p a t", a=2),
                                                g, ALU.mult).then_inc(pa_ev, 1)
                        dve.wait_ge(pa_ev, L * 4 + i + 1)
                        nc.vector.tensor_tensor(g, g, other, ALU.add).then_inc(m_done, 1)
                    for b in range(2):
                        i = 2 * j + b
                        dve.wait_ge(m_hi_done, L * 4 + i + 1)
                        nc.vector.tensor_tensor(h_lo[:, 2 * i:2 * i + 2, :], gates[:, 2 * i:2 * i + 2, :],
                                                h_hi[:, 2 * i:2 * i + 2, :].bitcast(F32),
                                                ALU.subtract).then_inc(m_lo_done, 1)

                def o_low():
                    for b in range(2):
                        dve.wait_ge(o_hi_done, L * 2 + b + 1)
                        nc.vector.tensor_tensor(o_lo[:, 2 * b:2 * b + 2, :],
                                                bank[4 + b][:, :].rearrange("p (a t) -> p a t", a=2),
                                                o_hi[:, 2 * b:2 * b + 2, :].bitcast(F32),
                                                ALU.subtract).then_inc(o_lo_done, 1)

                def residual(c, src, gate):
                    nc.vector.scalar_tensor_tensor(x[:, c, :], src, mod[:, gate + c:gate + c + 1], x[:, c, :],
                                                   op0=ALU.mult, op1=ALU.add).then_inc(x_upd, 1)

                for n in range(N_FFN):
                    turn = n - N_ATTEND
                    if 0 <= turn - 1 < HEADS:
                        scores(turn - 1)
                    if n >= 2 and ada_group_after(n - 2) is not None:
                        mod_columns(ada_group_after(n - 2), 1, bank[7][:, 0:4])
                    if n == 18:
                        centre()
                    if n == 19:
                        ln_tail()
                    split(n + LOOKAHEAD)
                    if n in (2, 4):
                        qk_scale(n // 2 - 1)
                    if n in (N_CONV + 2, N_CONV + 4):
                        glu_half((n - N_CONV) // 2 - 1)
                    conv_steps(n)
                    if n == 17:
                        o_low()
                    if 0 <= turn - 1 < HEADS:
                        inverse(turn - 1)
                    if n in (1, 3):
                        qk_sums(n // 2)
                    if n == 18:
                        mean_square(1, CONV_CH, 6)
                        diagonal(1)
                        merge_b(0)
                    if n == 19:
                        ln_silu()
                        merge_b(1)
                    if N_PA <= n < N_WO:
                        merge_a(n - N_PA)
                    if N_WO <= n < N_FFN:
                        if n == N_WO:
                            dve.wait_ge(mod_done, L * ADA_GROUPS + ADA_GROUPS - ADA_LAST)
                            norm_gain(1)
                        for t in range(2):
                            c = 2 * (n - N_WO) + t
                            if n < N_FFN - 1 or t == 1:
                                dve.wait_ge(used, L * N_SPLIT + n + 1)
                            else:
                                dve.wait_ge(bank_mm, L * 8 + 5)
                            b, cols = wo_place(n - N_WO, t)
                            residual(c, bank[b][:, cols], M_GA1)
                mean_square(2, D, 4)
                diagonal(2)
                split(N_FFN + 2)
                scale_x(1)
                low_h(1)
                mod_columns(ADA_GROUPS - ADA_LAST, ADA_LAST, bank[5][:, 0:4 * ADA_LAST])
                split(N_FFN + 3)

                def at(base, col):
                    if isinstance(col, int):
                        return vec[:, base + col:base + col + 1]
                    return vec[:, bass.ds(col + base, 1)]

                def ffn(i, parity):
                    done = 0
                    for tap in (1, 0):
                        back = 2 - tap
                        for s in range(2):
                            for t in range(2):
                                if tap == 1:
                                    dve.wait_ge(u_ev, L * 4 * PAIRS + i * 4 + 2 * s + 2)
                                else:
                                    dve.wait_ge(u_conv, L * 8 * PAIRS + i * 8 + done - 3)
                                col = 2 * i + t + s * (KF // 2)
                                dst = u[:, 2 * s + t, back:T]
                                nc.vector.scalar_tensor_tensor(
                                    dst, bank[2 * parity + s][:, t * T:(t + 1) * T - back],
                                    at(V_FW + tap * KF, col), dst,
                                    op0=ALU.mult, op1=ALU.add).then_inc(u_conv, 1)
                                done += 1
                    dve.wait_ge(u_silu, L * PAIRS + i + 1)
                    nc.vector.tensor_tensor(u[:, 0:2, :], u[:, 0:2, :], u[:, 2:4, :], ALU.mult).then_inc(f_done, 1)
                    dve.wait_ge(f_hi_done, L * PAIRS + i + 1)
                    nc.vector.tensor_tensor(f_lo[:, parity, :, :], u[:, 0:2, :],
                                            f_hi[:, parity, :, :].bitcast(F32), ALU.subtract).then_inc(f_lo_done, 1)

                ffn(0, 0)

                def ffn_round(it, last):
                    for j in range(2):
                        base = N_FFN + 2 + 3 * j
                        split(base + 2, it=it)
                        split(base + 3, it=it)
                        if not (last and j == 1):
                            split(base + 4, it=it)
                        ffn(it * 2 + (1 + j), (1 + j) % 2)

                with dve.Fori(0, (PAIRS - 1) // 2 - 1) as it:
                    ffn_round(it, False)
                ffn_round((PAIRS - 1) // 2 - 1, True)
                for c in range(KD):
                    if c < KD - 2:
                        dve.wait_ge(bank_mm, L * 8 + 6 + c // 2)
                    else:
                        dve.wait_ge(used, L * N_SPLIT + N_SPLIT)
                    residual(c, bank[4 + c // 2][:, (c % 2) * T:(c % 2 + 1) * T], M_GA2)

        @block.tensor
        def _(pe):
            pe.wait_ge(ld_small[5], 16)
            pe.wait_ge(rel_done, 1)
            nc.tensor.matmul(bank[0][0:HEADS, 0:TABLE], rel[:, :], onehot[:, :], start=True,
                             stop=True).then_inc(table_mm, 1)
            pe.wait_ge(table_ev, 1)
            pe.wait_ge(cond_done, 1)
            pe.wait_ge(ld_small[3], 16)
            pe.wait_ge(ld_small[6], 16)
            pe.wait_ge(bias_in, 32)
            for i in range(4):
                part = (acc, lin)[i // 2][:, 2 * (i % 2):2 * (i % 2) + 2, :]
                last = nc.tensor.matmul(bank[i][:, :], flip[:, :], part.rearrange("p a t -> p (a t)"),
                                        start=True, stop=True)
            last.then_inc(bias_mm, 1)
            pe.wait_ge(bias_done, 1)
            with pe.Fori(0, DEPTH) as L:
                def three(dst, lo_slot, hi_slot, cols, a_hi_, a_lo_, first, last, check=True):
                    nc.tensor.matmul(dst, hi_slot[:, cols], a_hi_, start=first, stop=False,
                                     skip_group_check=not check)
                    nc.tensor.matmul(dst, hi_slot[:, cols], a_lo_, start=False, stop=False,
                                     skip_group_check=not check)
                    return nc.tensor.matmul(dst, lo_slot[:, cols], a_hi_, start=False, stop=last,
                                            skip_group_check=not check)

                def chunk(n, banks, a_hi_, a_lo_, ks, each=None, early=False, between=None):
                    slot = n % SPLIT_SLOTS
                    width = CH // ks
                    pe.wait_ge(lo_done, L * N_SPLIT + n + 1 + RAW_SLOTS)
                    for t in range(width // P):
                        for k in range(ks):
                            if each and t == 0:
                                each(k)
                            col = k * width + t * P
                            last = three(bank[banks[t // 2]][:, (t % 2) * T:(t % 2 + 1) * T], w_lo[slot],
                                         w_hi[slot], slice(col, col + P), a_hi_[:, k, :], a_lo_[:, k, :],
                                         k == 0, k == ks - 1)
                        if t == 1 and early:
                            last.then_inc(bank_mm, 1)
                        if t == 1 and between:
                            between()
                    last.then_inc(used, 1)

                def chunk_by_k(n, b, a_hi_, a_lo_, each):
                    slot = n % SPLIT_SLOTS
                    pe.wait_ge(lo_done, L * N_SPLIT + n + 1 + RAW_SLOTS)
                    for k in range(KD):
                        each(k)
                        for t in range(2):
                            col = k * 2 * P + t * P
                            last = three(bank[b][:, t * T:(t + 1) * T], w_lo[slot], w_hi[slot],
                                         slice(col, col + P), a_hi_[:, k, :], a_lo_[:, k, :],
                                         k == 0 and t == 0, k == KD - 1, check=False)
                    last.then_inc(used, 1)

                def wo_last(n):
                    slot = n % SPLIT_SLOTS
                    pe.wait_ge(lo_done, L * N_SPLIT + n + 1 + RAW_SLOTS)
                    for t in range(2):
                        b, cols = wo_place(n - N_WO, t)
                        for k in range(KD):
                            col = k * 2 * P + t * P
                            last = three(bank[b][:, cols], w_lo[slot], w_hi[slot], slice(col, col + P),
                                         h_hi[:, k, :], h_lo[:, k, :], k == 0, k == KD - 1)
                        last.then_inc((bank_mm, used)[t], 1)

                def token_chunk(n, m, half):
                    slot = n % SPLIT_SLOTS
                    pe.wait_ge(lo_done, L * N_SPLIT + n + 1 + RAW_SLOTS)
                    b = 2 * m % 4
                    for kk in range(4):
                        k = 4 * half + kk
                        if n == N_QKV or n == N_QKV + 1:
                            pe.wait_ge(lo_h, L * 16 + k + 1)
                        w = slice(kk * 512, (kk + 1) * 512)
                        for tt in range(TT):
                            tok = slice(tt * P, (tt + 1) * P)
                            dst = bank[b + tt][:, :]
                            nc.tensor.matmul(dst, h_hi[:, k, tok], w_hi[slot][:, w], start=(k == 0), stop=False)
                            nc.tensor.matmul(dst, h_lo[:, k, tok], w_hi[slot][:, w], start=False, stop=False)
                            last = nc.tensor.matmul(dst, h_hi[:, k, tok], w_lo[slot][:, w], start=False,
                                                    stop=(k == KD - 1))
                    last.then_inc(used, 1)

                def ada_rows(g, b):
                    for half in range(2):
                        r = RAW_OF[("ada", 2 * g + half)]
                        pe.wait_ge(raw_full[r % RAW_SLOTS], raw_need(L, r))
                        for kk in range(4):
                            last = nc.tensor.matmul(bank[b][32 * kk:32 * kk + 32, :], cond[:, 4 * half + kk, :],
                                                    raw[r % RAW_SLOTS][:, kk * 512:(kk + 1) * 512],
                                                    start=(half == 0), stop=(half == 1))
                        last.then_inc(ada_used, 1)

                def turn_rows(g):
                    pe.wait_ge(row_ev, L * ADA_GROUPS + g + 1)
                    if g < ADA_FIRST:
                        rows, dst = ada_rows_a[:, g, :], bank[6][:, 4 * g:4 * g + 4]
                    elif g < ADA_GROUPS - ADA_LAST:
                        rows, dst = ada_rows_b, bank[7][:, 0:4]
                    else:
                        at = 4 * (g - ADA_GROUPS + ADA_LAST)
                        rows, dst = (ada_rows_b if at == 0 else ada_rows_c), bank[5][:, at:at + 4]
                    for q in range(4):
                        last = nc.tensor.matmul(dst[:, q:q + 1], rows[:, q * P:(q + 1) * P], ones[:, 0:1],
                                                start=True, stop=True)
                    last.then_inc(modt, 1)

                def sum_squares(i, src, tiles, b):
                    for c in range(tiles):
                        if i == 1:
                            pe.wait_ge(sq_ln, L + 1)
                        else:
                            pe.wait_ge(sq_x, L * 8 + (i // 2) * 4 + c // 2 + 1)
                        for tt in range(TT):
                            last = nc.tensor.matmul(bank[b][:, 256 + tt:257 + tt], src[:, c, tt * P:(tt + 1) * P],
                                                    ones[:, 0:1], start=(c == 0 and tt == 0), stop=(c == tiles - 1),
                                                    skip_group_check=True)
                    last.then_inc(stat_mm, 1)

                def spread(i, b):
                    pe.wait_ge(diag_done, L * 3 + i + 1)
                    for tt in range(TT):
                        last = nc.tensor.matmul(bank[b][:, tt * P:(tt + 1) * P], ones[:, :], diag[:, tt, :],
                                                start=True, stop=True)
                    last.then_inc(bcast, 1)

                def transposes(src, sem_):
                    for b in range(2):
                        for a in range(2):
                            for tt in range(TT):
                                cc = 2 * b + a
                                last = nc.tensor.transpose(bank[4 + b][:, a * T + tt * P:a * T + (tt + 1) * P],
                                                           src[:, tt, cc * P:(cc + 1) * P], ident[:, :])
                        last.then_inc(sem_, 1)

                def attend(t):
                    if t < HEADS:
                        if t >= 1:
                            pe.wait_ge(s_ev, L * HEADS + t)
                        part = slice((t % 2) * HD, (t % 2 + 1) * HD)
                        qh, kh = qT[part, t // 2, :], kT[part, t // 2, :]
                        nc.tensor.matmul(bank[4][:, 0:P], qh[:, 0:P], kh[:, 0:P], start=True, stop=True)
                        nc.tensor.matmul(bank[4][:, P:3 * P], qh[:, P:T], kh[:, :], start=True,
                                         stop=True).then_inc(s_mm, 1)
                    if t >= 1:
                        if t >= 2:
                            pe.wait_ge(pt_ev, L * (HEADS + 1) + t - 1)
                            hh = t - 2
                            p_of = pT[:, hh % 2, :]
                            cols = slice(hh * HD, (hh + 1) * HD)
                            nc.tensor.matmul(bank[5][:, 3 * P:3 * P + HD], p_of[:, 0:P], v_tok[:, 0, cols],
                                             start=True, stop=True)
                            nc.tensor.matmul(bank[5][:, 3 * P + HD:4 * P], p_of[:, P:2 * P], v_tok[:, 0, cols],
                                             start=True, stop=False)
                            last = nc.tensor.matmul(bank[5][:, 3 * P + HD:4 * P], p_of[:, 2 * P:3 * P],
                                                    v_tok[:, 1, cols], start=False, stop=True)
                        if t <= HEADS:
                            pe.wait_ge(exp_done, L * HEADS + t)
                            for i in range(3):
                                last = nc.tensor.transpose(bank[5][:, i * P:(i + 1) * P],
                                                           probs[:, (t - 1) % 2, i * P:(i + 1) * P], ident[:, :])
                        last.then_inc(pt_mm, 1)

                for g in range(ADA_FIRST - 1):
                    ada_rows(g, g)
                sum_squares(0, work, KD, 4)
                ada_rows(ADA_FIRST - 1, ADA_FIRST - 1)
                for g in range(ADA_FIRST - 1):
                    turn_rows(g)
                spread(0, 4)
                turn_rows(ADA_FIRST - 1)

                for n in range(N_FFN):
                    if n < N_CONV:
                        m, half = divmod(n - N_QKV, 2)
                        if n == N_QKV + 4:
                            pe.wait_ge(qk_norm, L * 2 * TT + TT)
                        token_chunk(n, m, half)
                    elif n < N_GATE:
                        if n == N_CONV:
                            pe.wait_ge(qk_norm, L * 2 * TT + 2 * TT)
                        if n == N_CONV + 2:
                            pe.wait_ge(v_ev, L * TT + TT)
                        chunk(n, [CONV_BANKS[n - N_CONV]], h_hi, h_lo, KD)
                    elif n < N_PB:
                        j = n - N_GATE
                        if j < 4:
                            pe.wait_ge(glu_done, L * 2 + j // 2 + 1)
                        else:
                            pe.wait_ge(gate_ev, L * 8 + j - 3)
                        chunk(n, [(2 + j) % 4], h_hi, h_lo, KD)
                    elif n < N_PA:
                        j = n - N_PB
                        pe.wait_ge(gate_ev, L * 8 + 6 + 2 * j)
                        pe.wait_ge(o_lo_done, L * 2 + 2)
                        chunk(n, [(2 + 2 * j) % 4, (3 + 2 * j) % 4], o_hi, o_lo, KC, early=True,
                              between=(lambda: sum_squares(1, lin, KC, 6)) if j == 0 else None)
                    elif n < N_WO:
                        j = n - N_PA
                        pe.wait_ge(pb_ev, L * 4 + 2 + 2 * j)

                        def a_ready(k):
                            pe.wait_ge(a_lo_done, L * KC + k + 1)
                        chunk(n, [(2 + 2 * j) % 4, (3 + 2 * j) % 4], a_hi, a_lo, KC,
                              a_ready if j == 0 else None, early=True)
                    else:
                        j = n - N_WO
                        pe.wait_ge(pa_ev, L * 4 + (2 if j < 2 else 4))
                        if j == 0:
                            def m_ready(k):
                                pe.wait_ge(m_lo_done, L * 4 + 1 + k // 2)
                            chunk_by_k(n, 2, h_hi, h_lo, m_ready)
                        elif j < 3:
                            chunk(n, [(2 + j) % 4], h_hi, h_lo, KD)
                        else:
                            wo_last(n)

                    g = ada_group_after(n)
                    if g is not None:
                        pe.wait_ge(mod_done, L * ADA_GROUPS + g)
                        ada_rows(g, 7)
                    elif n >= 1 and ada_group_after(n - 1) is not None:
                        turn_rows(ada_group_after(n - 1))
                    if n == 3:
                        pe.wait_ge(qk_norm, L * 2 * TT + TT)
                        transposes(q_tok, qk_tr)
                    if n == 5:
                        pe.wait_ge(qk_norm, L * 2 * TT + 2 * TT)
                        pe.wait_ge(qk_ev, L * 4 + 2)
                        transposes(k_tok, qk_tr)
                    if n == N_ATTEND:
                        pe.wait_ge(qk_ev, L * 4 + 4)
                    if 0 <= n - N_ATTEND < HEADS + 2:
                        attend(n - N_ATTEND)
                    if n == 16:
                        pe.wait_ge(pt_ev, L * (HEADS + 1) + HEADS + 1)
                        transposes(o_tok, o_tr)
                    if n == 17:
                        pe.wait_ge(conv, (L + 1) * len(CONV_OPS))
                        for t in range(KC):
                            last = nc.tensor.matmul(bank[6][:, 0:T], ones[:, :], acc[:, t, :], start=(t == 0),
                                                    stop=(t == KC - 1))
                        last.then_inc(mean_mm, 1)
                    if n == 18:
                        spread(1, 6)

                ada_rows(ADA_GROUPS - 2, 7)
                sum_squares(2, work, KD, 4)
                pe.wait_ge(cn_done, L + 1)
                ada_rows(ADA_GROUPS - 1, 6)
                spread(2, 4)
                turn_rows(ADA_GROUPS - 2)
                turn_rows(ADA_GROUPS - 1)

                def up_ready(k):
                    pe.wait_ge(lo_h, L * 16 + 8 + k + 1)

                def down(n, slot, i, parity, by_bank=False):
                    pe.wait_ge(lo_done, L * N_SPLIT + n + (1 + RAW_SLOTS))
                    pe.wait_ge(f_lo_done, L * PAIRS + i + 1)
                    for o in range(KD):
                        for kk in range(2):
                            col = kk * D + o * P
                            last = three(bank[4 + o // 2][:, (o % 2) * T:(o % 2 + 1) * T], w_lo[slot], w_hi[slot],
                                         slice(col, col + P), f_hi[:, parity, kk, :], f_lo[:, parity, kk, :],
                                         False, False, check=False)
                        if by_bank and o % 2 == 1 and o < KD - 1:
                            last.then_inc(bank_mm, 1)
                    last.then_inc(used, 1)

                chunk_by_k(N_FFN, 0, h_hi, h_lo, up_ready)
                chunk(N_FFN + 1, [1], h_hi, h_lo, KD)
                pe.wait_ge(mod_done, L * ADA_GROUPS + ADA_GROUPS)
                for b in range(4, 8):
                    nc.tensor.matmul(bank[b][:, :], zeros[:, 0:P], zeros[:, :], start=True, stop=True)

                with pe.Fori(0, (PAIRS - 1) // 2) as it:
                    for j in range(2):
                        i = it * 2 + (1 + j)
                        parity = (1 + j) % 2
                        base = N_FFN + 2 + 3 * j
                        for s in range(2):
                            slot = (base + s) % SPLIT_SLOTS
                            pe.wait_ge(lo_done, L * N_SPLIT + it * RAW_SLOTS + (base + s + 1 + RAW_SLOTS))
                            if s == 0:
                                pe.wait_ge(f_done, L * PAIRS + it * 2 + (j + 1))
                            for t in range(2):
                                for k in range(KD):
                                    col = k * 2 * P + t * P
                                    last = three(bank[2 * parity + s][:, t * T:(t + 1) * T], w_lo[slot], w_hi[slot],
                                                 slice(col, col + P), h_hi[:, k, :], h_lo[:, k, :],
                                                 k == 0, k == KD - 1)
                            last.then_inc(used, 1)
                        down(it * RAW_SLOTS + (base + 2), (base + 2) % SPLIT_SLOTS, it * 2 + j, j % 2)
                down(N_SPLIT - 1, (N_SPLIT - 1) % SPLIT_SLOTS, PAIRS - 1, (PAIRS - 1) % 2, by_bank=True)


def _stream(w):
    chunks = []

    def tall(m, rows, cols):
        b = m[rows, cols]
        return b.reshape(b.shape[0] // P, P, b.shape[1]).transpose(1, 0, 2).reshape(P, CH)

    every = slice(None)
    for l in range(DEPTH):
        w_in = w["w_in"][l]
        for kind, n in ORDER:
            if kind == "ada":
                g, half = divmod(n, 2)
                c = tall(w["ada_w"][l], slice(half * 512, half * 512 + 512), slice(g * 512, g * 512 + 512))
            elif n < N_CONV:
                m, half = divmod(n - N_QKV, 2)
                at = 2 * CONV_CH + m * 512
                c = tall(w_in, slice(half * 512, half * 512 + 512), slice(at, at + 512))
            elif n < N_GATE:
                j, gate = divmod(n - N_CONV, 2)
                at = gate * CONV_CH + j * 256
                c = tall(w_in, every, slice(at, at + 256))
            elif n < N_PB:
                at = 2 * CONV_CH + 3 * HEADS * HD + (n - N_GATE) * 256
                c = tall(w_in, every, slice(at, at + 256))
            elif n < N_WO:
                name = "w_pb" if n < N_PA else "w_pa"
                j = (n - N_PB) % 2
                c = tall(w[name][l], every, slice(j * 512, j * 512 + 512))
            elif n < N_FFN:
                at = (n - N_WO) * 256
                c = tall(w["w_o"][l], every, slice(at, at + 256))
            else:
                f = n - N_FFN
                if f < 2:
                    what, i = f, 0
                elif n == N_SPLIT - 1:
                    what, i = 2, PAIRS - 1
                else:
                    i, what = divmod(f - 2, 3)
                    i += what < 2
                if what < 2:
                    at = what * D_FF + i * 256
                    c = tall(w["w_up"][l], every, slice(at, at + 256))
                else:
                    c = tall(w["w_down"][l], slice(i * 256, i * 256 + 256), every)
            chunks.append(c)
    return np.stack(chunks)


def _packs(w):
    out = np.empty((P, DEPTH, NV), np.float32)

    def put(l, at, v):
        cols = v.reshape(-1, P).T
        out[:, l, at:at + cols.shape[1]] = cols

    for l in range(DEPTH):
        put(l, V_G1, w["norm1_g"][l])
        put(l, V_G2, w["norm2_g"][l])
        put(l, V_CW, w["conv_w"][l])
        put(l, V_CB, w["conv_b"][l])
        put(l, V_LG, w["conv_ln_g"][l])
        put(l, V_LB, w["conv_ln_b"][l])
        put(l, V_QG, np.concatenate([w["q_norm_g"][l]] * 2))
        put(l, V_KG, np.concatenate([w["k_norm_g"][l]] * 2))
        put(l, V_FW, w["ffn_conv_w"][l])
        put(l, V_FB, w["ffn_conv_b"][l])
        put(l, V_AB, w["ada_b"][l])
    return out


def _onehot():
    hot = np.zeros((BUCKETS + 1, TABLE), np.float32)
    exact = BUCKETS // 2
    for i in range(TABLE):
        dist = T - 1 - i
        if dist < 0:
            b = BUCKETS
        elif dist < exact:
            b = dist
        else:
            b = min(exact + int(math.log(dist / exact) / math.log(MAX_DISTANCE / exact) * (BUCKETS - exact)),
                    BUCKETS - 1)
        hot[b, i] = 1.0
    return hot


def kernel(**inputs):
    import concourse.bacc as bacc
    from concourse.bass_utils import run_bass_kernel_spmd

    w = {k: np.asarray(v) for k, v in inputs.items()}
    arrays = {
        "stream": _stream(w),
        "x": np.ascontiguousarray(w["x"][0].reshape(T, KD, P).transpose(2, 1, 0)),
        "c": np.ascontiguousarray(w["c"][0].reshape(KD, P).T),
        "packs": _packs(w),
        "rel": np.ascontiguousarray(w["rel_bias"].T),
        "onehot": _onehot(),
        "ident": np.eye(P, dtype=np.float32),
        "flip": np.ascontiguousarray(np.eye(P, dtype=np.float32)[::-1]),
    }
    nc = bacc.Bacc("TRN2", target_bir_lowering=False, num_devices=1)
    args = [nc.dram_tensor(f"in_{n}", a.shape, F32, kind="ExternalInput").ap() for n, a in arrays.items()]
    out = nc.dram_tensor("out_x", (P, KD, T), F32, kind="ExternalOutput").ap()
    trunk(nc, *args, out)
    r = run_bass_kernel_spmd(nc, [{f"in_{n}": a for n, a in arrays.items()}], core_ids=[0])
    got = r.results[0]["out_x"]
    return got.transpose(2, 1, 0).reshape(1, T, D)
```

```python
import math
from contextlib import ExitStack

import numpy as np

import concourse.bass as bass
from concourse import mybir

F32 = mybir.dt.float32
F32R = mybir.dt.float32r
BF16 = mybir.dt.bfloat16
ALU = mybir.AluOpType
ACT = mybir.ActivationFunctionType
AX = mybir.AxisListType

P = 128
D = 1024
T = 256
DEPTH = 2
CONV_CH = D // 2
TAPS = 31
HD = 64
HEADS = (D // 2) // HD
BUCKETS = 32
MAX_DISTANCE = 2048
D_FF = ((int(8 * D / 3) + 255) // 256) * 256
FTAPS = 3
EPS = 1e-6
KD = D // P
KC = CONV_CH // P
TT = T // P
PAIRS = D_FF // (2 * P)
KF = 2 * D_FF // P
CH = 2048
MASKED = -1.0e30

QKV = (0, 1, 4, 5, 6, 7)
CONV = (2, 3, 8, 9)
N_GATE = 10
N_PB = 18
N_PA = 20
N_WO = 22
N_FFN = 26
N_SPLIT = N_FFN + 3 * PAIRS
ADA_GROUPS = 6 * D // 512
ADA_FIRST = 4
ADA_LAST = 2
ADA_AFTER = 7
N_ADA = 2 * ADA_GROUPS
BATCHES = ((0, 1), (2, 3), tuple(range(ADA_FIRST, ADA_GROUPS - ADA_LAST)),
           tuple(range(ADA_GROUPS - ADA_LAST, ADA_GROUPS)))
N_BATCH = len(BATCHES)
MOST = max(len(batch) for batch in BATCHES)
BATCH_OF = {g: i for i, batch in enumerate(BATCHES) for g in batch}
ADA_COLUMNS = (0, 2, 1, 3) + tuple(range(ADA_FIRST, ADA_GROUPS))
RAW_SLOTS = 6
SPLIT_SLOTS = 3
LOOKAHEAD = 2


def ada_group_after(n):
    g = ADA_FIRST + (n - ADA_AFTER) // 2
    if n >= ADA_AFTER and (n - ADA_AFTER) % 2 == 0 and g < ADA_GROUPS - ADA_LAST:
        return g
    return None


def stream_order():
    order = [("ada", a) for a in range(2 * ADA_FIRST)]
    order.insert(ADA_FIRST, ("split", 0))
    for n in range(N_SPLIT):
        if n > 0:
            order.append(("split", n))
        g = ada_group_after(n - LOOKAHEAD)
        if g is not None:
            order += [("ada", 2 * g), ("ada", 2 * g + 1)]
        if n - LOOKAHEAD == N_FFN - 1:
            order += [("ada", a) for a in range(2 * (ADA_GROUPS - ADA_LAST), 2 * ADA_GROUPS)]
    return order


ORDER = stream_order()
N_RAW = len(ORDER)
RAW_OF = {what: r for r, what in enumerate(ORDER)}
FFN_ROUNDS = (PAIRS - 1) // 2
R_LOOP = RAW_OF[("split", N_FFN + 2)] + RAW_SLOTS
USES = [sum(r % RAW_SLOTS == s for r in range(N_RAW)) for s in range(RAW_SLOTS)]

V_G1 = 0
V_G2 = V_G1 + KD
V_CW = V_G2 + KD
V_CB = V_CW + TAPS * KC
V_LG = V_CB + KC
V_LB = V_LG + KC
V_QG = V_LB + KC
V_KG = V_QG + 1
V_FW = V_KG + 1
V_FB = V_FW + FTAPS * KF
V_AB = V_FB + KF
NV = V_AB + 6 * KD
M_GA1, M_SH2, M_SC2, M_GA2 = (KD * i for i in range(2, 6))


def m_shift(i, c):
    return M_SH2 + c if i else c // 4 * 8 + c % 4


TABLE = 2 * T - P - 1
CONV_OPS = [(tap, t) for half in (0, 2) for tap in range(TAPS) for t in (half, half + 1)]
CONV_FROM = 4
CONV_SHARES = [8, 0, 4, 12, 14, 10, 10, 10, 10, 10, 9, 9, 9, 9]
N_ATTEND = 7
CONV_BANKS = (2, 3, 0, 1)


def conv_share(n):
    at = n - CONV_FROM
    if not 0 <= at < len(CONV_SHARES):
        return []
    return range(sum(CONV_SHARES[:at]), sum(CONV_SHARES[:at + 1]))


assert sum(CONV_SHARES) == len(CONV_OPS)


def trunk(nc, stream, x_in, c_in, packs_in, rel_in, onehot_in, ident_in, out):
    ctx = ExitStack()
    with ctx:
        def sb(name, shape, dt=F32):
            return ctx.enter_context(nc.sbuf_tensor(name, shape, dt))

        def sem(name):
            return ctx.enter_context(nc.semaphore(name))

        raw = [sb(f"raw{i}", [P, CH]) for i in range(RAW_SLOTS)]
        w_hi = [sb(f"w_hi{i}", [P, CH], F32R) for i in range(SPLIT_SLOTS)]
        w_lo = [sb(f"w_lo{i}", [P, CH], F32R) for i in range(SPLIT_SLOTS)]
        x = sb("x", [P, KD, T])
        h_hi = sb("h_hi", [P, KD, T], F32R)
        h_lo = sb("h_lo", [P, KD, T], F32R)
        work = sb("work", [P, KD, T])
        q_tok = work[:, 0:4, :].rearrange("p (a b) t -> p a (b t)", a=TT)
        k_tok = work[:, 4:8, :].rearrange("p (a b) t -> p a (b t)", a=TT)
        gates = sb("gates", [P, 2 * KD, T])
        ada_rows_a = gates[:, 0:4, :].rearrange("p (a b) t -> p a (b t)", a=2)
        ada_rows_b = sb("ada_rows_b", [P, 512])
        glu = sb("glu", [P, KC, TAPS - 1 + T])
        acc = sb("acc", [P, KC, T])
        lin = sb("lin", [P, KC, T])
        a_hi = sb("a_hi", [P, KC, T], F32R)
        a_lo = sb("a_lo", [P, KC, T], F32R)
        o_hi = sb("o_hi", [P, KC, T], F32R)
        o_lo = sb("o_lo", [P, KC, T], F32R)
        v_tok = sb("v_tok", [P, TT, 512])
        qT = sb("qT", [P, KC, T])
        kT = sb("kT", [P, KC, T])
        bias = sb("bias", [P, HEADS, T])
        probs = k_tok[:, :, 0:3 * P]
        pT = sb("pT", [P, 2, 3 * P])
        o_tok = q_tok
        u = gates[:, 0:4, :]
        f_hi = a_hi[:, :, :].rearrange("p (a b) t -> p a b t", a=2)
        f_lo = a_lo[:, :, :].rearrange("p (a b) t -> p a b t", a=2)
        packs = sb("packs", [P, DEPTH, NV])
        vec = sb("vec", [P, NV])
        mod = sb("mod", [P, 6 * KD])
        gs = sb("gs", [P, 2, KD])
        qg8 = sb("qg8", [P, 1])
        cT = sb("cT", [P, KD])
        cond = sb("cond", [P, KD, MOST - 1 + 32])
        sel = sb("sel", [P, MOST])
        ident = sb("ident", [P, P])
        ones = sb("ones", [P, P])
        zeros = sb("zeros", [P, 512], BF16)
        neg_half = sb("neg_half", [P, 16])
        stat = sb("stat", [P, TT])
        rstd = sb("rstd", [P, TT])
        diag = sb("diag", [P, TT, P])
        qk_stat = sb("qk_stat", [P, 2, TT * HEADS])
        qk_rstd = sb("qk_rstd", [P, 2, TT * HEADS])
        row_max = sb("row_max", [P, HEADS, TT])
        row_sum = sb("row_sum", [P, HEADS, TT])
        row_inv = sb("row_inv", [P, HEADS, TT])
        rel = sb("rel", [BUCKETS + 1, HEADS])
        onehot = gates[0:BUCKETS + 1, 8:10, :].rearrange("p a t -> p (a t)")[:, 0:TABLE]
        table = gates[0:HEADS, 10:12, :].rearrange("p a t -> p (a t)")[:, 0:TABLE]
        table_dram = nc.dram_tensor("table_scratch", (HEADS, TABLE), F32, kind="Internal").ap()

        def bias_of(h, cols):
            whole = bias[:, h, :]
            return bass.AP(tensor=whole.tensor, offset=whole.offset + T - 1 - cols.start,
                           ap=[whole.ap[0], [-1, cols.stop - cols.start]])

        bank = [ctx.enter_context(nc.psum_tensor(f"bank{i}", [P, 512], F32)) for i in range(8)]

        raw_full = [sem(f"raw_full{i}") for i in range(RAW_SLOTS)]
        hi_done = sem("hi_done")
        lo_done = sem("lo_done")
        used = sem("used")
        ada_used = sem("ada_used")
        row_ev = sem("row_ev")
        modt = sem("modt")
        mod_done = sem("mod_done")
        vec_done = sem("vec_done")
        gs_done = sem("gs_done")
        sq_x = sem("sq_x")
        sq_add = sem("sq_add")
        sq_ln = sem("sq_ln")
        stat_mm = sem("stat_mm")
        stat_ev = sem("stat_ev")
        rstd_done = sem("rstd_done")
        diag_done = sem("diag_done")
        bcast = sem("bcast")
        xn_done = sem("xn_done")
        hi_h = sem("hi_h")
        aff_h = sem("aff_h")
        lo_h = sem("lo_h")
        bank_mm = sem("bank_mm")
        cg_sig = sem("cg_sig")
        glu_done = sem("glu_done")
        conv = sem("conv")
        mean_mm = sem("mean_mm")
        cen_done = sem("cen_done")
        cn_done = sem("cn_done")
        ln_sig = sem("ln_sig")
        ln_aff = sem("ln_aff")
        a_done = sem("a_done")
        a_hi_done = sem("a_hi_done")
        a_lo_done = sem("a_lo_done")
        qk_sq = sem("qk_sq")
        qk_red = sem("qk_red")
        qk_mean = sem("qk_mean")
        qk_pow = sem("qk_pow")
        qk_norm = sem("qk_norm")
        qk_tr = sem("qk_tr")
        qk_ev = sem("qk_ev")
        v_ev = sem("v_ev")
        gate_ev = sem("gate_ev")
        gate_sig = sem("gate_sig")
        s_mm = sem("s_mm")
        s_ev = sem("s_ev")
        max_done = sem("max_done")
        max_raw = sem("max_raw")
        exp_done = sem("exp_done")
        inv_done = sem("inv_done")
        pt_mm = sem("pt_mm")
        pt_ev = sem("pt_ev")
        o_tr = sem("o_tr")
        o_hi_done = sem("o_hi_done")
        o_lo_done = sem("o_lo_done")
        pa_ev = sem("pa_ev")
        pb_ev = sem("pb_ev")
        m_done = sem("m_done")
        m_hi_done = sem("m_hi_done")
        m_lo_done = sem("m_lo_done")
        x_upd = sem("x_upd")
        u_ev = sem("u_ev")
        u_conv = sem("u_conv")
        u_silu = sem("u_silu")
        f_done = sem("f_done")
        f_hi_done = sem("f_hi_done")
        f_lo_done = sem("f_lo_done")
        bias_in = sem("bias_in")
        ld_small = [sem(f"ld_small{i}") for i in range(6)]
        sel_done = sem("sel_done")
        const_done = sem("const_done")
        cond_done = sem("cond_done")
        rel_done = sem("rel_done")
        table_mm = sem("table_mm")
        table_ev = sem("table_ev")
        table_out = sem("table_out")
        table_asked = sem("table_asked")
        stored = sem("stored")

        def raw_need(L, r, uses_more=0):
            return L * (16 * USES[r % RAW_SLOTS]) + (16 * (r // RAW_SLOTS + 1) + 16 * uses_more)

        def wo_place(j, t):
            if (j, t) == (3, 1):
                return 5, slice(0, T)
            return (2 + j) % 4, slice(t * T, (t + 1) * T)

        block = ctx.enter_context(nc.Block())

        @block.sync
        def _(sp):
            def fetch(r_of_all, slot):
                sp.dma_start(raw[slot][:, :], stream[r_of_all, :, :]).then_inc(raw_full[slot], 16)

            def load(L, r):
                before = r - RAW_SLOTS
                lower = 0
                if before < 0:
                    before = max(q for q in range(N_RAW) if q % RAW_SLOTS == r % RAW_SLOTS)
                    lower = N_SPLIT
                kind, n = ORDER[before]
                if kind == "split":
                    sp.wait_ge(lo_done, L * N_SPLIT + (n + 1 - lower + RAW_SLOTS))
                else:
                    sp.wait_ge(ada_used, L * N_ADA + (n + 1))
                fetch(L * N_RAW + r, r % RAW_SLOTS)

            sp.dma_start(x[:, :, :], x_in).then_inc(ld_small[0], 16)
            sp.dma_start(cT[:, :], c_in).then_inc(ld_small[1], 16)
            sp.dma_start(packs[:, :, :], packs_in).then_inc(ld_small[2], 16)
            with sp.Fori(0, DEPTH) as L:
                for r in range(R_LOOP):
                    if r == 2:
                        sp.wait_ge(table_asked, 1)
                    load(L, r)
                    if r == RAW_OF[("split", 2)]:
                        sp.wait_ge(table_out, 16)
                        skewed = bass.AP(tensor=table_dram.tensor, offset=0,
                                         ap=[[1, P], [TABLE, HEADS], [1, T]])
                        sp.dma_start(bias[:, :, :], skewed).then_inc(bias_in, 16)
                with sp.Fori(0, FFN_ROUNDS - 1) as it:
                    for j in range(RAW_SLOTS):
                        sp.wait_ge(lo_done, L * N_SPLIT + it * RAW_SLOTS
                                   + (ORDER[R_LOOP + j - RAW_SLOTS][1] + 1 + RAW_SLOTS))
                        fetch(L * N_RAW + it * RAW_SLOTS + (R_LOOP + j), (R_LOOP + j) % RAW_SLOTS)
                load(L, N_RAW - 1)
            for c in range(0, KD, 2):
                sp.wait_ge(x_upd, 2 * DEPTH * KD + c + 2)
                sp.dma_start(out[:, c:c + 2, :], x[:, c:c + 2, :]).then_inc(stored, 16)
            sp.wait_ge(stored, 16 * (KD // 2))

        @block.gpsimd
        def _(pool):
            nc.gpsimd.memset(ones[:, :], 1.0)
            nc.gpsimd.memset(neg_half[:, :], -0.5)
            nc.gpsimd.memset(zeros[:, :], 0.0)
            nc.gpsimd.memset(glu[:, :, 0:TAPS - 1], 0.0)
            nc.gpsimd.memset(cond[:, :, :], 0.0).then_inc(const_done, 1)
            pool.wait_ge(table_ev, 1)
            pool.dma_start(table_dram, table[:, :]).then_inc(table_out, 16)
            pool.sem_inc(table_asked, 1)
            pool.wait_ge(ld_small[2], 16)
            with pool.Fori(0, DEPTH) as L:
                pool.wait_ge(x_upd, L * (2 * KD) + KD)
                nc.gpsimd.tensor_copy(vec[:, :], packs[:, L, :]).then_inc(vec_done, 1)

                def power(i):
                    pool.wait_ge(stat_ev, L * 3 + (i + 1))
                    nc.gpsimd.tensor_tensor(rstd[:, :], stat[:, :], neg_half[:, 0:TT],
                                            ALU.pow).then_inc(rstd_done, 1)

                power(0)
                for m in range(2):
                    pool.wait_ge(qk_mean, L * 2 + (m + 1))
                    nc.gpsimd.tensor_tensor(qk_rstd[:, m, :], qk_stat[:, m, :], neg_half[:, :],
                                            ALU.pow).then_inc(qk_pow, 1)
                power(1)
                power(2)

        @block.scalar
        def _(act):
            act.dma_start(ident[:, :], ident_in).then_inc(ld_small[3], 16)
            act.dma_start(rel[0:BUCKETS, :], rel_in).then_inc(ld_small[4], 16)
            act.dma_start(onehot[:, :], onehot_in).then_inc(ld_small[5], 16)
            act.wait_ge(ld_small[1], 16)
            act.wait_ge(const_done, 1)
            nc.scalar.activation(cond[:, :, MOST - 1], cT[:, :], ACT.Silu).then_inc(cond_done, 1)
            with act.Fori(0, DEPTH) as L:
                def split(n, it=0):
                    slot = n % SPLIT_SLOTS
                    r = RAW_OF[("split", n)]
                    act.wait_ge(raw_full[r % RAW_SLOTS], raw_need(L, r, it))
                    if n >= SPLIT_SLOTS:
                        act.wait_ge(used, L * N_SPLIT + it * RAW_SLOTS + (n + 1 - SPLIT_SLOTS))
                    nc.scalar.activation(w_hi[slot][:, :], raw[r % RAW_SLOTS][:, :],
                                         ACT.Copy).then_inc(hi_done, 1)

                def rows(i):
                    act.wait_ge(ada_used, L * N_ADA + 2 * (BATCHES[i][-1] + 1))
                    if i >= 2:
                        act.wait_ge(modt, L * N_BATCH + i)
                    dst, src = ((ada_rows_a[:, 0, :], bank[2]), (ada_rows_a[:, 1, :], bank[3]),
                                (ada_rows_b[:, :], bank[7]), (ada_rows_b[:, :], bank[7]))[i]
                    nc.scalar.activation(dst, src[:, :], ACT.Copy).then_inc(row_ev, 1)

                def squares(i):
                    for c in range(0, KD, 2):
                        act.wait_ge(x_upd, L * (2 * KD) + (i * KD + c + 2))
                        nc.scalar.activation(work[:, c:c + 2, :], x[:, c:c + 2, :],
                                             ACT.Square).then_inc(sq_x, 1)

                def high_h(i, half):
                    act.wait_ge(gs_done, L * 4 + (2 + half if i == 0 else 4))
                    for c in range(4 * half, 4 * half + 4):
                        act.wait_ge(xn_done, L * 8 + i * 4 + c // 2 + 1)
                        shift = m_shift(i, c)
                        nc.scalar.activation(h_hi[:, c, :], work[:, c, :], ACT.Identity,
                                             bias=mod[:, shift:shift + 1],
                                             scale=gs[:, i, c:c + 1]).then_inc(hi_h, 1)

                squares(0)
                split(0)
                rows(0)
                high_h(0, 0)
                rows(1)
                split(1)
                high_h(0, 1)

                def conv_gate(j):
                    act.wait_ge(used, L * N_SPLIT + CONV[2 * j + 1] + 1)
                    if j == 0:
                        act.wait_ge(modt, L * N_BATCH + 2)
                    nc.scalar.activation(gates[:, 2 * j:2 * j + 2, :],
                                         bank[CONV_BANKS[2 * j + 1]][:, :].rearrange("p (a t) -> p a t", a=2),
                                         ACT.Sigmoid).then_inc(cg_sig, 1)

                def qk_squares(m):
                    act.wait_ge(used, L * N_SPLIT + QKV[2 * m + 1] + 1)
                    for tt in range(TT):
                        if m == 1:
                            act.wait_ge(qk_red, L * 2 * TT + tt + 1)
                        nc.scalar.activation(lin[:, 2 * tt:2 * tt + 2, :],
                                             bank[tt][:, :].rearrange("p (a t) -> p a t", a=2),
                                             ACT.Square).then_inc(qk_sq, 1)

                def qk_copy(m):
                    if m == 0:
                        act.wait_ge(gs_done, L * 4 + 1)
                    for b in range(2):
                        act.wait_ge(qk_tr, L * 4 + 2 * m + b + 1)
                        dst = (qT if m == 0 else kT)[:, 2 * b:2 * b + 2, :]
                        gain = qg8[:, 0:1] if m == 0 else vec[:, V_KG:V_KG + 1]
                        nc.scalar.activation(dst, bank[4 + b][:, :].rearrange("p (a t) -> p a t", a=2),
                                             ACT.Copy, scale=gain).then_inc(qk_ev, 1)

                def v_copy():
                    act.wait_ge(used, L * N_SPLIT + QKV[5] + 1)
                    for tt in range(TT):
                        nc.scalar.activation(v_tok[:, tt, :], bank[2 + tt][:, :], ACT.Copy).then_inc(v_ev, 1)

                def gate_copy(j, func):
                    act.wait_ge(used, L * N_SPLIT + N_GATE + j + 1)
                    if j < 2:
                        act.wait_ge(glu_done, L * 2 + 2)
                    nc.scalar.activation(gates[:, 2 * j:2 * j + 2, :],
                                         bank[(2 + j) % 4][:, :].rearrange("p (a t) -> p a t", a=2),
                                         func).then_inc(gate_ev, 1)

                def exponentials(t):
                    act.wait_ge(max_done, L * HEADS + t + 1)
                    nc.scalar.activation(probs[:, t % 2, 0:P], probs[:, t % 2, 0:P], ACT.Exp,
                                         bias=row_max[:, t, 0:1], accum_out=row_sum[:, t, 0:1])
                    nc.scalar.activation(probs[:, t % 2, P:3 * P], probs[:, t % 2, P:3 * P], ACT.Exp,
                                         bias=row_max[:, t, 1:2],
                                         accum_out=row_sum[:, t, 1:2]).then_inc(exp_done, 1)

                def attend(t):
                    act.wait_ge(pt_mm, L * (HEADS + 1) + t)
                    if t >= 2:
                        hh = t - 2
                        act.wait_ge(inv_done, L * HEADS + hh + 1)
                        for tt in range(TT):
                            last = nc.scalar.activation(
                                o_tok[:, tt, hh * HD:(hh + 1) * HD],
                                bank[5][:, 3 * P + tt * HD:3 * P + (tt + 1) * HD],
                                ACT.Copy, scale=row_inv[:, hh, tt:tt + 1])
                    if t <= HEADS:
                        last = nc.scalar.activation(pT[:, (t - 1) % 2, :], bank[5][:, 0:3 * P], ACT.Copy)
                    last.then_inc(pt_ev, 1)

                def ln_squares():
                    act.wait_ge(cen_done, L + 1)
                    nc.scalar.activation(lin[:, :, :], acc[:, :, :], ACT.Square).then_inc(sq_ln, 1)

                def ln_tail():
                    act.wait_ge(cn_done, L + 1)
                    for t in range(KC):
                        nc.scalar.activation(lin[:, t, :], acc[:, t, :], ACT.Sigmoid,
                                             bias=vec[:, V_LB + t:V_LB + t + 1],
                                             scale=vec[:, V_LG + t:V_LG + t + 1]).then_inc(ln_sig, 1)
                    for t in range(KC):
                        act.wait_ge(a_done, L * KC + t + 1)
                        nc.scalar.activation(a_hi[:, t, :], acc[:, t, :], ACT.Copy).then_inc(a_hi_done, 1)

                def gate_sigmoids():
                    for part in (gates[:, 0:KD, :], gates[:, KD:KD + 2, :]):
                        nc.scalar.activation(part, part, ACT.Sigmoid).then_inc(gate_sig, 1)

                def o_high():
                    for b in range(2):
                        act.wait_ge(o_tr, L * 2 + b + 1)
                        nc.scalar.activation(o_hi[:, 2 * b:2 * b + 2, :],
                                             bank[4 + b][:, :].rearrange("p (a t) -> p a t", a=2),
                                             ACT.Copy).then_inc(o_hi_done, 1)

                def m_high(i):
                    act.wait_ge(m_done, L * 4 + i + 1)
                    nc.scalar.activation(h_hi[:, 2 * i:2 * i + 2, :], gates[:, 2 * i:2 * i + 2, :],
                                         ACT.Copy).then_inc(m_hi_done, 1)

                for n in range(N_FFN):
                    turn = n - N_ATTEND
                    if n == 18:
                        ln_squares()
                    split(n + LOOKAHEAD)
                    if n == 4:
                        qk_copy(0)
                    if n == 7:
                        qk_copy(1)
                    if n == 16:
                        gate_sigmoids()
                    if n == 17:
                        o_high()
                    if n == 19:
                        ln_tail()
                    if 0 <= turn - 1 < HEADS:
                        exponentials(turn - 1)
                    if n in (QKV[1], QKV[3]):
                        qk_squares(QKV.index(n) // 2)
                    if n == QKV[5]:
                        v_copy()
                    if n in (CONV[1], CONV[3]):
                        conv_gate(CONV.index(n) // 2)
                    if N_GATE <= n < N_PB:
                        gate_copy(n - N_GATE, ACT.Copy if n < 15 else ACT.Sigmoid)
                    if ada_group_after(n) == BATCHES[2][-1]:
                        rows(2)
                    if 1 <= turn <= HEADS + 1:
                        attend(turn)
                    if N_PA <= n < N_WO:
                        m_high(2 * (n - N_PA))
                        m_high(2 * (n - N_PA) + 1)
                squares(1)
                high_h(1, 0)
                high_h(1, 1)
                rows(3)
                split(N_FFN + 2)
                split(N_FFN + 3)

                def ffn(i, first, parity, opening=False):
                    for s in range(2):
                        act.wait_ge(used, L * N_SPLIT + (first + s + 1))
                        if s == 0 and not opening:
                            act.wait_ge(f_lo_done, L * 2 * PAIRS + i * 2)
                        for t in range(2):
                            col = 2 * i + t + s * (KF // 2)
                            b = bank[2 * parity + s]
                            nc.scalar.activation(u[:, 2 * s + t, :], b[:, t * T:(t + 1) * T], ACT.Identity,
                                                 bias=at(V_FB, col), scale=at(V_FW + 2 * KF, col)).then_inc(u_ev, 1)
                    for t in range(2):
                        act.wait_ge(u_conv, L * 8 * PAIRS + i * 8 + 7 + t)
                        nc.scalar.activation(u[:, 2 + t, :], u[:, 2 + t, :], ACT.Silu).then_inc(u_silu, 1)
                    for t in range(2):
                        act.wait_ge(f_done, L * 2 * PAIRS + i * 2 + t + 3)
                        nc.scalar.activation(f_hi[:, parity, t, :], u[:, t, :], ACT.Copy).then_inc(f_hi_done, 1)

                def at(base, col):
                    if isinstance(col, int):
                        return vec[:, base + col:base + col + 1]
                    return vec[:, bass.ds(col + base, 1)]

                ffn(0, N_FFN, 0, opening=True)

                def ffn_round(it, last):
                    for j in range(2):
                        base = N_FFN + 2 + 3 * j
                        split(base + 2, it=it)
                        if last and j == 1:
                            split(base + 3, it=it)
                        else:
                            split(base + 3, it=it)
                            split(base + 4, it=it)
                        i = it * 2 + (1 + j)
                        ffn(i, it * RAW_SLOTS + base, (1 + j) % 2)

                with act.Fori(0, (PAIRS - 1) // 2 - 1) as it:
                    ffn_round(it, False)
                ffn_round((PAIRS - 1) // 2 - 1, True)

        @block.vector
        def _(dve):
            dve.sem_inc(lo_done, RAW_SLOTS)
            dve.sem_inc(f_done, 2)
            dve.wait_ge(ld_small[4], 16)
            nc.vector.memset(rel[BUCKETS:BUCKETS + 1, :], MASKED).then_inc(rel_done, 1)
            dve.wait_ge(table_mm, 1)
            nc.vector.tensor_copy(table[:, :], bank[0][0:HEADS, 0:TABLE]).then_inc(table_ev, 1)
            dve.wait_ge(ld_small[0], 16)
            dve.sem_inc(x_upd, KD)
            dve.wait_ge(ld_small[3], 16)
            nc.vector.reduce_sum(sel[:, :], ident[:, :].rearrange("p (k i) -> p i k", i=32)[:, 0:MOST, :],
                                 AX.X).then_inc(sel_done, 1)
            with dve.Fori(0, DEPTH) as L:
                def split(n, it=0):
                    slot = n % SPLIT_SLOTS
                    r = RAW_OF[("split", n)]
                    dve.wait_ge(hi_done, L * N_SPLIT + it * RAW_SLOTS + n + 1)
                    nc.vector.tensor_tensor(w_lo[slot][:, :], raw[r % RAW_SLOTS][:, :],
                                            w_hi[slot][:, :].bitcast(F32), ALU.subtract).then_inc(lo_done, 1)

                def add_squares(i, k):
                    dve.wait_ge(sq_x, L * 8 + 4 * i + k + 1)
                    if k == 2:
                        dve.wait_ge(sq_add, L * 3 + 1)
                    nc.vector.tensor_tensor(work[:, 0:2, :], work[:, 0:2, :], work[:, 2 * k:2 * k + 2, :],
                                            ALU.add).then_inc(sq_add, 1)

                def mean_square(i, width, b):
                    dve.wait_ge(stat_mm, L * 3 + i + 1)
                    nc.vector.tensor_scalar(stat[:, :], bank[b][:, 256:256 + TT], 1.0 / width, EPS,
                                            ALU.mult, ALU.add).then_inc(stat_ev, 1)

                def diagonal(i):
                    dve.wait_ge(rstd_done, L * 3 + i + 1)
                    for tt in range(TT):
                        last = nc.vector.tensor_scalar(diag[:, tt, :], ident[:, :], rstd[:, tt:tt + 1], None,
                                                       ALU.mult)
                    last.then_inc(diag_done, 1)

                def scale_x(i, pair):
                    if pair == 0:
                        dve.wait_ge(bcast, L * 3 + (1 if i == 0 else 3))
                    c = 2 * pair
                    nc.vector.tensor_tensor(work[:, c:c + 2, :], x[:, c:c + 2, :],
                                            bank[4][:, 0:T].unsqueeze(1).broadcast_to((P, 2, T)),
                                            ALU.mult).then_inc(xn_done, 1)

                def norm_gain(i, half=None):
                    if i == 0:
                        sc, dst = mod[:, 8 * half + 4:8 * half + 8], slice(4 * half, 4 * half + 4)
                    else:
                        sc, dst = mod[:, M_SC2:M_SC2 + KD], slice(0, KD)
                    g = vec[:, (V_G2 if i else V_G1) + dst.start:(V_G2 if i else V_G1) + dst.stop]
                    nc.vector.scalar_tensor_tensor(gs[:, i, dst], sc, 1.0, g,
                                                   op0=ALU.add, op1=ALU.mult).then_inc(gs_done, 1)

                def low_h(i, pair):
                    tiles = (2 * pair, 2 * pair + 1)
                    for c in tiles:
                        shift = m_shift(i, c)
                        dve.wait_ge(hi_h, L * 16 + i * 8 + c + 1)
                        nc.vector.tensor_scalar(work[:, c, :], work[:, c, :], gs[:, i, c:c + 1],
                                                mod[:, shift:shift + 1], ALU.mult, ALU.add).then_inc(aff_h, 1)
                    for c in tiles:
                        dve.wait_ge(aff_h, L * 16 + i * 8 + c + 1)
                        nc.vector.tensor_tensor(h_lo[:, c, :], work[:, c, :], h_hi[:, c, :].bitcast(F32),
                                                ALU.subtract).then_inc(lo_h, 1)

                def mod_columns(i, src):
                    dve.wait_ge(modt, L * N_BATCH + i + 1)
                    count = len(BATCHES[i])
                    at = 4 * BATCHES[i][0]

                    def by_group(columns):
                        return columns[:, at:at + 4 * count].rearrange("p (g q) -> p g q", q=4)
                    nc.vector.tensor_tensor(by_group(mod), src.rearrange("p (q g) -> p g q", q=4),
                                            by_group(vec[:, V_AB:V_AB + 6 * KD]), ALU.add).then_inc(mod_done, 1)

                add_squares(0, 1)
                add_squares(0, 2)
                split(0)
                mean_square(0, D, 4)
                dve.wait_ge(vec_done, L + 1)
                nc.vector.tensor_scalar(qg8[:, :], vec[:, V_QG:V_QG + 1], HD ** -0.5, None,
                                        ALU.mult).then_inc(gs_done, 1)
                for half in range(2):
                    mod_columns(half, bank[6][:, 8 * half:8 * half + 8])
                    dve.wait_ge(mod_done, L * N_BATCH + half + 1)
                    norm_gain(0, half)
                    if half == 0:
                        diagonal(0)
                        scale_x(0, 0)
                        scale_x(0, 1)
                        low_h(0, 0)
                        scale_x(0, 2)
                        low_h(0, 1)
                        scale_x(0, 3)
                    else:
                        split(1)
                        low_h(0, 2)
                        low_h(0, 3)

                def glu_half(j):
                    dve.wait_ge(cg_sig, L * 2 + j + 1)
                    nc.vector.tensor_tensor(glu[:, 2 * j:2 * j + 2, TAPS - 1:],
                                            bank[CONV_BANKS[2 * j]][:, :].rearrange("p (a t) -> p a t", a=2),
                                            gates[:, 2 * j:2 * j + 2, :], ALU.mult).then_inc(glu_done, 1)

                def conv_steps(n):
                    for i in conv_share(n):
                        tap, t = CONV_OPS[i]
                        w = vec[:, V_CW + tap * KC + t:V_CW + tap * KC + t + 1]
                        src = glu[:, t, tap:tap + T]
                        if tap == 0:
                            dve.wait_ge(glu_done, L * 2 + t // 2 + 1)
                            nc.vector.tensor_scalar(acc[:, t, :], src, w, vec[:, V_CB + t:V_CB + t + 1],
                                                    ALU.mult, ALU.add).then_inc(conv, 1)
                        else:
                            dve.wait_ge(conv, L * len(CONV_OPS) + i - 1)
                            nc.vector.scalar_tensor_tensor(acc[:, t, :], src, w, acc[:, t, :],
                                                           op0=ALU.mult, op1=ALU.add).then_inc(conv, 1)

                def qk_sums(m):
                    for tt in range(TT):
                        dve.wait_ge(qk_sq, L * 2 * TT + m * TT + tt + 1)
                        nc.vector.reduce_sum(qk_stat[:, m, tt * HEADS:(tt + 1) * HEADS],
                                             lin[:, 2 * tt:2 * tt + 2, :].rearrange("p a (h d) -> p (a h) d", d=HD),
                                             AX.X).then_inc(qk_red, 1)
                    dve.wait_ge(qk_red, L * 2 * TT + (m + 1) * TT)
                    nc.vector.tensor_scalar(qk_stat[:, m, :], qk_stat[:, m, :], 1.0 / HD, EPS,
                                            ALU.mult, ALU.add).then_inc(qk_mean, 1)

                def qk_scale(m):
                    dve.wait_ge(qk_pow, L * 2 + m + 1)
                    for tt in range(TT):
                        dst = (q_tok if m == 0 else k_tok)[:, tt, :]
                        r = qk_rstd[:, m, tt * HEADS:(tt + 1) * HEADS]
                        nc.vector.tensor_tensor(dst.rearrange("p (h d) -> p h d", d=HD),
                                                bank[tt][:, :].rearrange("p (h d) -> p h d", d=HD),
                                                r.unsqueeze(2).broadcast_to((P, HEADS, HD)),
                                                ALU.mult).then_inc(qk_norm, 1)

                def scores(t):
                    if t == 0:
                        dve.wait_ge(bias_in, L * 16 + 16)
                    dve.wait_ge(s_mm, L * HEADS + t + 1)
                    if t >= 2:
                        dve.wait_ge(pt_mm, L * (HEADS + 1) + t - 1)
                    nc.vector.tensor_tensor(probs[:, t % 2, 0:P], bank[4 + 2 * (t % 2)][:, 0:P],
                                            bias_of(t, slice(P, T)), ALU.add)
                    nc.vector.tensor_tensor(probs[:, t % 2, P:3 * P], bank[4 + 2 * (t % 2)][:, P:3 * P],
                                            bias_of(t, slice(0, T)), ALU.add).then_inc(s_ev, 1)
                    dve.wait_ge(s_ev, L * HEADS + t + 1)
                    nc.vector.reduce_max(row_max[:, t, 0:1], probs[:, t % 2, 0:P], AX.X)
                    nc.vector.reduce_max(row_max[:, t, 1:2], probs[:, t % 2, P:3 * P], AX.X).then_inc(max_raw, 1)
                    dve.wait_ge(max_raw, L * HEADS + t + 1)
                    nc.vector.tensor_scalar(row_max[:, t, :], row_max[:, t, :], -1.0, None,
                                            ALU.mult).then_inc(max_done, 1)

                def inverse(t):
                    dve.wait_ge(exp_done, L * HEADS + t + 1)
                    nc.vector.reciprocal(row_inv[:, t, :], row_sum[:, t, :]).then_inc(inv_done, 1)

                def centre():
                    dve.wait_ge(mean_mm, L + 1)
                    nc.vector.scalar_tensor_tensor(
                        acc[:, :, :], bank[6][:, 0:T].unsqueeze(1).broadcast_to((P, KC, T)),
                        -1.0 / CONV_CH, acc[:, :, :], op0=ALU.mult, op1=ALU.add).then_inc(cen_done, 1)

                def ln_tail():
                    dve.wait_ge(bcast, L * 3 + 2)
                    nc.vector.tensor_tensor(acc[:, :, :], acc[:, :, :],
                                            bank[6][:, 0:T].unsqueeze(1).broadcast_to((P, KC, T)),
                                            ALU.mult).then_inc(cn_done, 1)

                def ln_silu():
                    for t in range(KC + 2):
                        if t < KC:
                            dve.wait_ge(ln_sig, L * KC + t + 1)
                            nc.vector.tensor_scalar(acc[:, t, :], acc[:, t, :], vec[:, V_LG + t:V_LG + t + 1],
                                                    vec[:, V_LB + t:V_LB + t + 1],
                                                    ALU.mult, ALU.add).then_inc(ln_aff, 1)
                        if t >= 2:
                            dve.wait_ge(a_hi_done, L * KC + t - 1)
                            nc.vector.tensor_tensor(a_lo[:, t - 2, :], acc[:, t - 2, :],
                                                    a_hi[:, t - 2, :].bitcast(F32),
                                                    ALU.subtract).then_inc(a_lo_done, 1)
                        if 1 <= t <= KC:
                            dve.wait_ge(ln_aff, L * KC + t)
                            nc.vector.tensor_tensor(acc[:, t - 1, :], acc[:, t - 1, :], lin[:, t - 1, :],
                                                    ALU.mult).then_inc(a_done, 1)

                def merge_b(j):
                    if j == 0:
                        dve.wait_ge(gate_sig, L * 2 + 2)
                        dve.wait_ge(gate_ev, L * 8 + 8)
                    for b in range(2):
                        ready(N_PB + j, 2 * b + 1, j)
                        g = gates[:, KD + 4 * j + 2 * b:KD + 4 * j + 2 * b + 2, :]
                        nc.vector.tensor_tensor(g, bank[(2 + 2 * j + b) % 4][:, :].rearrange("p (a t) -> p a t", a=2),
                                                g, ALU.mult).then_inc(pb_ev, 1)

                def ready(n, tiles, early):
                    if tiles == 1:
                        dve.wait_ge(bank_mm, L * 8 + early + 1)
                    else:
                        dve.wait_ge(used, L * N_SPLIT + n + 1)

                def merge_product(i):
                    ready(N_PA + i // 2, 2 * (i % 2) + 1, 2 + i // 2)
                    g = gates[:, 2 * i:2 * i + 2, :]
                    nc.vector.tensor_tensor(g, bank[(2 + i) % 4][:, :].rearrange("p (a t) -> p a t", a=2),
                                            g, ALU.mult).then_inc(pa_ev, 1)

                def merge_sum(i):
                    g, other = gates[:, 2 * i:2 * i + 2, :], gates[:, KD + 2 * i:KD + 2 * i + 2, :]
                    dve.wait_ge(pa_ev, L * 4 + i + 1)
                    nc.vector.tensor_tensor(g, g, other, ALU.add).then_inc(m_done, 1)

                def merge_low(i):
                    dve.wait_ge(m_hi_done, L * 4 + i + 1)
                    nc.vector.tensor_tensor(h_lo[:, 2 * i:2 * i + 2, :], gates[:, 2 * i:2 * i + 2, :],
                                            h_hi[:, 2 * i:2 * i + 2, :].bitcast(F32),
                                            ALU.subtract).then_inc(m_lo_done, 1)

                def o_low():
                    for b in range(2):
                        dve.wait_ge(o_hi_done, L * 2 + b + 1)
                        nc.vector.tensor_tensor(o_lo[:, 2 * b:2 * b + 2, :],
                                                bank[4 + b][:, :].rearrange("p (a t) -> p a t", a=2),
                                                o_hi[:, 2 * b:2 * b + 2, :].bitcast(F32),
                                                ALU.subtract).then_inc(o_lo_done, 1)

                def residual(c, src, gate):
                    nc.vector.scalar_tensor_tensor(x[:, c, :], src, mod[:, gate + c:gate + c + 1], x[:, c, :],
                                                   op0=ALU.mult, op1=ALU.add).then_inc(x_upd, 1)

                for n in range(N_FFN):
                    turn = n - N_ATTEND
                    if 0 <= turn - 1 < HEADS:
                        scores(turn - 1)
                    if ada_group_after(n - 2) == BATCHES[2][-1]:
                        mod_columns(2, bank[7][:, 0:4 * len(BATCHES[2])])
                    if n == 18:
                        centre()
                    if n == 19:
                        ln_tail()
                    if N_PA <= n < N_WO:
                        i = 2 * (n - N_PA)
                        merge_product(i)
                        merge_sum(i)
                        merge_product(i + 1)
                        merge_low(i)
                        merge_sum(i + 1)
                        if n > N_PA:
                            merge_low(i + 1)
                    split(n + LOOKAHEAD)
                    if n == N_PA:
                        merge_low(1)
                    if n - 1 in (QKV[1], QKV[3]):
                        qk_scale(QKV.index(n - 1) // 2)
                    if n - 1 in (CONV[1], CONV[3]):
                        glu_half(CONV.index(n - 1) // 2)
                    conv_steps(n)
                    if n == 17:
                        o_low()
                    if 0 <= turn - 1 < HEADS:
                        inverse(turn - 1)
                    if n in (QKV[1], QKV[3]):
                        qk_sums(QKV.index(n) // 2)
                    if n == 18:
                        mean_square(1, CONV_CH, 6)
                        diagonal(1)
                        merge_b(0)
                    if n == 19:
                        ln_silu()
                        merge_b(1)
                    if N_WO <= n < N_FFN:
                        if n == N_WO:
                            dve.wait_ge(mod_done, L * N_BATCH + 3)
                            norm_gain(1)
                        for t in range(2):
                            c = 2 * (n - N_WO) + t
                            if n < N_FFN - 1 or t == 1:
                                dve.wait_ge(used, L * N_SPLIT + n + 1)
                            else:
                                dve.wait_ge(bank_mm, L * 8 + 5)
                            if c == 6:
                                add_squares(1, 1)
                            b, cols = wo_place(n - N_WO, t)
                            residual(c, bank[b][:, cols], M_GA1)
                mean_square(2, D, 4)
                diagonal(2)
                scale_x(1, 0)
                for pair in range(KD // 2):
                    if pair < KD // 2 - 1:
                        scale_x(1, pair + 1)
                    low_h(1, pair)
                split(N_FFN + 2)
                mod_columns(3, bank[5][:, 0:4 * ADA_LAST])
                split(N_FFN + 3)

                def at(base, col):
                    if isinstance(col, int):
                        return vec[:, base + col:base + col + 1]
                    return vec[:, bass.ds(col + base, 1)]

                def ffn(i, parity):
                    done = 0
                    for s in range(2):
                        for tap in (1, 0):
                            back = 2 - tap
                            for t in range(2):
                                if tap == 1:
                                    dve.wait_ge(u_ev, L * 4 * PAIRS + i * 4 + 2 * s + 2)
                                else:
                                    dve.wait_ge(u_conv, L * 8 * PAIRS + i * 8 + done - 1)
                                col = 2 * i + t + s * (KF // 2)
                                dst = u[:, 2 * s + t, back:T]
                                nc.vector.scalar_tensor_tensor(
                                    dst, bank[2 * parity + s][:, t * T:(t + 1) * T - back],
                                    at(V_FW + tap * KF, col), dst,
                                    op0=ALU.mult, op1=ALU.add).then_inc(u_conv, 1)
                                done += 1
                    for t in range(2):
                        dve.wait_ge(u_silu, L * 2 * PAIRS + i * 2 + t + 1)
                        nc.vector.tensor_tensor(u[:, t, :], u[:, t, :], u[:, 2 + t, :],
                                                ALU.mult).then_inc(f_done, 1)
                    for t in range(2):
                        dve.wait_ge(f_hi_done, L * 2 * PAIRS + i * 2 + t + 1)
                        nc.vector.tensor_tensor(f_lo[:, parity, t, :], u[:, t, :],
                                                f_hi[:, parity, t, :].bitcast(F32),
                                                ALU.subtract).then_inc(f_lo_done, 1)

                ffn(0, 0)

                def ffn_round(it, last):
                    for j in range(2):
                        base = N_FFN + 2 + 3 * j
                        split(base + 2, it=it)
                        split(base + 3, it=it)
                        if not (last and j == 1):
                            split(base + 4, it=it)
                        ffn(it * 2 + (1 + j), (1 + j) % 2)

                with dve.Fori(0, (PAIRS - 1) // 2 - 1) as it:
                    ffn_round(it, False)
                ffn_round((PAIRS - 1) // 2 - 1, True)
                for c in range(KD):
                    if c < KD - 2:
                        dve.wait_ge(bank_mm, L * 8 + 6 + c // 2)
                    else:
                        dve.wait_ge(used, L * N_SPLIT + N_SPLIT)
                    residual(c, bank[4 + c // 2][:, (c % 2) * T:(c % 2 + 1) * T], M_GA2)

        @block.tensor
        def _(pe):
            pe.wait_ge(ld_small[5], 16)
            pe.wait_ge(rel_done, 1)
            nc.tensor.matmul(bank[0][0:HEADS, 0:TABLE], rel[:, :], onehot[:, :], start=True,
                             stop=True).then_inc(table_mm, 1)
            pe.wait_ge(table_ev, 1)
            pe.wait_ge(cond_done, 1)
            pe.wait_ge(sel_done, 1)
            with pe.Fori(0, DEPTH) as L:
                def three(dst, lo_slot, hi_slot, cols, a_hi_, a_lo_, first, last, check=True):
                    nc.tensor.matmul(dst, hi_slot[:, cols], a_hi_, start=first, stop=False,
                                     skip_group_check=not check)
                    nc.tensor.matmul(dst, hi_slot[:, cols], a_lo_, start=False, stop=False,
                                     skip_group_check=not check)
                    return nc.tensor.matmul(dst, lo_slot[:, cols], a_hi_, start=False, stop=last,
                                            skip_group_check=not check)

                def chunk(n, banks, a_hi_, a_lo_, ks, each=None, early=False, between=None):
                    slot = n % SPLIT_SLOTS
                    width = CH // ks
                    pe.wait_ge(lo_done, L * N_SPLIT + n + 1 + RAW_SLOTS)
                    for t in range(width // P):
                        for k in range(ks):
                            if each and t == 0:
                                each(k)
                            col = k * width + t * P
                            last = three(bank[banks[t // 2]][:, (t % 2) * T:(t % 2 + 1) * T], w_lo[slot],
                                         w_hi[slot], slice(col, col + P), a_hi_[:, k, :], a_lo_[:, k, :],
                                         k == 0, k == ks - 1)
                        if t == 1 and early:
                            last.then_inc(bank_mm, 1)
                        if t == 1 and between:
                            between()
                    last.then_inc(used, 1)

                def chunk_by_k(n, banks, a_hi_, a_lo_, ks, each):
                    slot = n % SPLIT_SLOTS
                    width = CH // ks
                    pe.wait_ge(lo_done, L * N_SPLIT + n + 1 + RAW_SLOTS)
                    for k in range(ks):
                        each(k)
                        for t in range(width // P):
                            col = k * width + t * P
                            last = three(bank[banks[t // 2]][:, (t % 2) * T:(t % 2 + 1) * T], w_lo[slot],
                                         w_hi[slot], slice(col, col + P), a_hi_[:, k, :], a_lo_[:, k, :],
                                         k == 0 and t % 2 == 0, k == ks - 1, check=False)
                            if t == 1 and k == ks - 1 and width // P > 2:
                                last.then_inc(bank_mm, 1)
                    last.then_inc(used, 1)

                def wo_last(n):
                    slot = n % SPLIT_SLOTS
                    pe.wait_ge(lo_done, L * N_SPLIT + n + 1 + RAW_SLOTS)
                    for t in range(2):
                        b, cols = wo_place(n - N_WO, t)
                        for k in range(KD):
                            col = k * 2 * P + t * P
                            last = three(bank[b][:, cols], w_lo[slot], w_hi[slot], slice(col, col + P),
                                         h_hi[:, k, :], h_lo[:, k, :], k == 0, k == KD - 1)
                        last.then_inc((bank_mm, used)[t], 1)

                def token_chunk(n, m, half, between=None):
                    slot = n % SPLIT_SLOTS
                    pe.wait_ge(lo_done, L * N_SPLIT + n + 1 + RAW_SLOTS)
                    b = (0, 0, 2)[m]
                    for kk in range(4):
                        k = 4 * half + kk
                        if kk == 1 and between:
                            between()
                        if m == 0:
                            pe.wait_ge(lo_h, L * 16 + k + 1)
                        w = slice(kk * 512, (kk + 1) * 512)
                        for tt in range(TT):
                            tok = slice(tt * P, (tt + 1) * P)
                            dst = bank[b + tt][:, :]
                            nc.tensor.matmul(dst, h_hi[:, k, tok], w_hi[slot][:, w], start=(k == 0), stop=False)
                            nc.tensor.matmul(dst, h_lo[:, k, tok], w_hi[slot][:, w], start=False, stop=False)
                            last = nc.tensor.matmul(dst, h_hi[:, k, tok], w_lo[slot][:, w], start=False,
                                                    stop=(k == KD - 1))
                    last.then_inc(used, 1)

                def ada_rows(g):
                    batch = BATCHES[BATCH_OF[g]]
                    i = batch.index(g)
                    b = (2, 3, 7, 7)[BATCH_OF[g]]
                    for half in range(2):
                        r = RAW_OF[("ada", 2 * g + half)]
                        pe.wait_ge(raw_full[r % RAW_SLOTS], raw_need(L, r))
                        for kk in range(4):
                            last = nc.tensor.matmul(bank[b][32 * kk:32 * kk + 32, :],
                                                    cond[:, 4 * half + kk, MOST - 1 - i:MOST + 31 - i],
                                                    raw[r % RAW_SLOTS][:, kk * 512:(kk + 1) * 512],
                                                    start=(i == 0 and half == 0),
                                                    stop=(g == batch[-1] and half == 1), skip_group_check=True)
                        last.then_inc(ada_used, 1)

                def turn_rows(i):
                    pe.wait_ge(row_ev, L * N_BATCH + i + 1)
                    count = len(BATCHES[i])
                    rows, dst = ((ada_rows_a[:, 0, :], bank[6][:, 0:8]), (ada_rows_a[:, 1, :], bank[6][:, 8:16]),
                                 (ada_rows_b, bank[7]), (ada_rows_b, bank[5]))[i]
                    for q in range(4):
                        last = nc.tensor.matmul(dst[:, q * count:(q + 1) * count], rows[:, q * P:(q + 1) * P],
                                                sel[:, 0:count], start=True, stop=True)
                    last.then_inc(modt, 1)

                def sum_squares(i, src, tiles, b, ready):
                    for c in tiles:
                        ready(c)
                        for tt in range(TT):
                            last = nc.tensor.matmul(bank[b][:, 256 + tt:257 + tt], src[:, c, tt * P:(tt + 1) * P],
                                                    ones[:, 0:1], start=(c == tiles[0] and tt == 0), stop=(c == tiles[-1]),
                                                    skip_group_check=True)
                    last.then_inc(stat_mm, 1)

                def sum_x_squares(i):
                    def ready(c):
                        if c < 2:
                            pe.wait_ge(sq_add, L * 3 + (2 if i == 0 else 3))
                        else:
                            pe.wait_ge(sq_x, L * 8 + 4 * i + c // 2 + 1)
                    sum_squares(2 * i, work, (0, 1, 6, 7) if i == 0 else (4, 5, 0, 1, 6, 7), 4, ready)

                def sum_ln_squares():
                    sum_squares(1, lin, range(KC), 6, lambda c: pe.wait_ge(sq_ln, L + 1))

                def spread(i, b):
                    pe.wait_ge(diag_done, L * 3 + i + 1)
                    for tt in range(TT):
                        last = nc.tensor.matmul(bank[b][:, tt * P:(tt + 1) * P], ones[:, :], diag[:, tt, :],
                                                start=True, stop=True)
                    last.then_inc(bcast, 1)

                def transposes(src, sem_):
                    for b in range(2):
                        for a in range(2):
                            for tt in range(TT):
                                cc = 2 * b + a
                                last = nc.tensor.transpose(bank[4 + b][:, a * T + tt * P:a * T + (tt + 1) * P],
                                                           src[:, tt, cc * P:(cc + 1) * P], ident[:, :])
                        last.then_inc(sem_, 1)

                def attend(t):
                    if t < HEADS and t % 2 == 0:
                        if t >= 2:
                            pe.wait_ge(s_ev, L * HEADS + t)
                        for q, keys, cols in ((slice(0, P), P, slice(0, P)), (slice(P, T), T, slice(P, 3 * P))):
                            for h in range(2):
                                part = slice(h * HD, (h + 1) * HD)
                                last = nc.tensor.matmul(bank[4 + 2 * h][:, cols], qT[part, t // 2, q],
                                                        kT[part, t // 2, 0:keys], start=True, stop=True)
                                if keys == T:
                                    last.then_inc(s_mm, 1)
                    if t >= 1:
                        if t >= 2:
                            pe.wait_ge(pt_ev, L * (HEADS + 1) + t - 1)
                            hh = t - 2
                            p_of = pT[:, hh % 2, :]
                            cols = slice(hh * HD, (hh + 1) * HD)
                            nc.tensor.matmul(bank[5][:, 3 * P:3 * P + HD], p_of[:, 0:P], v_tok[:, 0, cols],
                                             start=True, stop=True)
                            nc.tensor.matmul(bank[5][:, 3 * P + HD:4 * P], p_of[:, P:2 * P], v_tok[:, 0, cols],
                                             start=True, stop=False)
                            last = nc.tensor.matmul(bank[5][:, 3 * P + HD:4 * P], p_of[:, 2 * P:3 * P],
                                                    v_tok[:, 1, cols], start=False, stop=True)
                        if t <= HEADS:
                            pe.wait_ge(exp_done, L * HEADS + t)
                            for i in range(3):
                                last = nc.tensor.transpose(bank[5][:, i * P:(i + 1) * P],
                                                           probs[:, (t - 1) % 2, i * P:(i + 1) * P], ident[:, :])
                        last.then_inc(pt_mm, 1)

                ada_rows(0)
                ada_rows(1)
                sum_x_squares(0)
                turn_rows(0)
                ada_rows(2)
                spread(0, 4)
                ada_rows(3)

                for n in range(N_FFN):
                    if n in QKV:
                        m, half = divmod(QKV.index(n), 2)
                        if n == QKV[2]:
                            pe.wait_ge(qk_norm, L * 2 * TT + TT)
                        if n == QKV[4]:
                            pe.wait_ge(glu_done, L * 2 + 1)

                        def turn_k():
                            pe.wait_ge(qk_norm, L * 2 * TT + 2 * TT)
                            pe.wait_ge(qk_ev, L * 4 + 2)
                            transposes(k_tok, qk_tr)
                        token_chunk(n, m, half, {QKV[0]: lambda: turn_rows(1), QKV[5]: turn_k}.get(n))
                    elif n in CONV:
                        if n == CONV[2]:
                            pe.wait_ge(qk_norm, L * 2 * TT + 2 * TT)
                        chunk(n, [CONV_BANKS[CONV.index(n)]], h_hi, h_lo, KD)
                    elif n < N_PB:
                        j = n - N_GATE
                        if j < 2:
                            pe.wait_ge(v_ev, L * TT + TT)
                        elif j < 4:
                            pe.wait_ge(glu_done, L * 2 + 2)
                        else:
                            pe.wait_ge(gate_ev, L * 8 + j - 3)
                        chunk(n, [(2 + j) % 4], h_hi, h_lo, KD)
                    elif n < N_PA:
                        j = n - N_PB
                        pe.wait_ge(gate_ev, L * 8 + 6 + 2 * j)
                        pe.wait_ge(o_lo_done, L * 2 + 2)
                        chunk(n, [(2 + 2 * j) % 4, (3 + 2 * j) % 4], o_hi, o_lo, KC, early=True,
                              between=sum_ln_squares if j == 0 else None)
                    elif n < N_WO:
                        j = n - N_PA
                        pe.wait_ge(pb_ev, L * 4 + 2 + 2 * j)

                        def a_ready(k):
                            pe.wait_ge(a_lo_done, L * KC + k + 1)
                        if j == 0:
                            chunk_by_k(n, [2, 3], a_hi, a_lo, KC, a_ready)
                        else:
                            chunk(n, [0, 1], a_hi, a_lo, KC, early=True)
                    else:
                        j = n - N_WO
                        pe.wait_ge(pa_ev, L * 4 + (2 if j < 2 else 4))
                        if j == 0:
                            def m_ready(k):
                                pe.wait_ge(m_lo_done, L * 4 + 1 + k // 2)
                            chunk_by_k(n, [2], h_hi, h_lo, KD, m_ready)
                        elif j < 3:
                            chunk(n, [(2 + j) % 4], h_hi, h_lo, KD)
                        else:
                            wo_last(n)

                    g = ada_group_after(n)
                    if g is not None:
                        if g == BATCHES[2][0]:
                            pe.wait_ge(row_ev, L * N_BATCH + 2)
                        ada_rows(g)
                    elif ada_group_after(n - 1) == BATCHES[2][-1]:
                        turn_rows(2)
                    if n == 3:
                        pe.wait_ge(qk_norm, L * 2 * TT + TT)
                        transposes(q_tok, qk_tr)
                    if n == N_ATTEND:
                        pe.wait_ge(qk_ev, L * 4 + 4)
                    if n == N_ATTEND + 2:
                        pe.wait_ge(v_ev, L * TT + TT)
                    if 0 <= n - N_ATTEND < HEADS + 2:
                        attend(n - N_ATTEND)
                    if n == 17:
                        pe.wait_ge(pt_ev, L * (HEADS + 1) + HEADS + 1)
                        transposes(o_tok, o_tr)
                        pe.wait_ge(conv, (L + 1) * len(CONV_OPS))
                        for t in range(KC):
                            last = nc.tensor.matmul(bank[6][:, 0:T], ones[:, :], acc[:, t, :], start=(t == 0),
                                                    stop=(t == KC - 1))
                        last.then_inc(mean_mm, 1)
                    if n == 18:
                        spread(1, 6)

                sum_x_squares(1)
                pe.wait_ge(mod_done, L * N_BATCH + 3)
                ada_rows(BATCHES[3][0])
                spread(2, 4)
                ada_rows(BATCHES[3][1])

                def up_ready(k):
                    if k == KD - 1:
                        turn_rows(3)
                    pe.wait_ge(lo_h, L * 16 + 8 + k + 1)

                def down(n, slot, i, parity, by_bank=False):
                    pe.wait_ge(lo_done, L * N_SPLIT + n + (1 + RAW_SLOTS))
                    pe.wait_ge(f_lo_done, L * 2 * PAIRS + i * 2 + 2)
                    for o in range(KD):
                        for kk in range(2):
                            col = kk * D + o * P
                            last = three(bank[4 + o // 2][:, (o % 2) * T:(o % 2 + 1) * T], w_lo[slot], w_hi[slot],
                                         slice(col, col + P), f_hi[:, parity, kk, :], f_lo[:, parity, kk, :],
                                         False, False, check=False)
                        if by_bank and o % 2 == 1 and o < KD - 1:
                            last.then_inc(bank_mm, 1)
                    last.then_inc(used, 1)

                chunk_by_k(N_FFN, [0], h_hi, h_lo, KD, up_ready)
                chunk(N_FFN + 1, [1], h_hi, h_lo, KD)
                pe.wait_ge(mod_done, (L + 1) * N_BATCH)
                for b in range(4, 8):
                    nc.tensor.matmul(bank[b][:, :], zeros[:, 0:P], zeros[:, :], start=True, stop=True)

                with pe.Fori(0, (PAIRS - 1) // 2) as it:
                    for j in range(2):
                        i = it * 2 + (1 + j)
                        parity = (1 + j) % 2
                        base = N_FFN + 2 + 3 * j
                        for s in range(2):
                            slot = (base + s) % SPLIT_SLOTS
                            pe.wait_ge(lo_done, L * N_SPLIT + it * RAW_SLOTS + (base + s + 1 + RAW_SLOTS))
                            if s == 0:
                                pe.wait_ge(f_done, L * 2 * PAIRS + it * 4 + (2 * j + 2))
                            for t in range(2):
                                for k in range(KD):
                                    col = k * 2 * P + t * P
                                    last = three(bank[2 * parity + s][:, t * T:(t + 1) * T], w_lo[slot], w_hi[slot],
                                                 slice(col, col + P), h_hi[:, k, :], h_lo[:, k, :],
                                                 k == 0, k == KD - 1)
                            last.then_inc(used, 1)
                        down(it * RAW_SLOTS + (base + 2), (base + 2) % SPLIT_SLOTS, it * 2 + j, j % 2)
                down(N_SPLIT - 1, (N_SPLIT - 1) % SPLIT_SLOTS, PAIRS - 1, (PAIRS - 1) % 2, by_bank=True)


def _stream(w):
    chunks = []

    def tall(m, rows, cols):
        b = m[rows, cols]
        return b.reshape(b.shape[0] // P, P, b.shape[1]).transpose(1, 0, 2).reshape(P, CH)

    every = slice(None)
    for l in range(DEPTH):
        w_in = w["w_in"][l]
        for kind, n in ORDER:
            if kind == "ada":
                g, half = divmod(n, 2)
                at = ADA_COLUMNS[g] * 512
                c = tall(w["ada_w"][l], slice(half * 512, half * 512 + 512), slice(at, at + 512))
            elif n in QKV:
                m, half = divmod(QKV.index(n), 2)
                at = 2 * CONV_CH + m * 512
                c = tall(w_in, slice(half * 512, half * 512 + 512), slice(at, at + 512))
            elif n in CONV:
                j, gate = divmod(CONV.index(n), 2)
                at = gate * CONV_CH + j * 256
                c = tall(w_in, every, slice(at, at + 256))
            elif n < N_PB:
                at = 2 * CONV_CH + 3 * HEADS * HD + (n - N_GATE) * 256
                c = tall(w_in, every, slice(at, at + 256))
            elif n < N_WO:
                name = "w_pb" if n < N_PA else "w_pa"
                j = (n - N_PB) % 2
                c = tall(w[name][l], every, slice(j * 512, j * 512 + 512))
            elif n < N_FFN:
                at = (n - N_WO) * 256
                c = tall(w["w_o"][l], every, slice(at, at + 256))
            else:
                f = n - N_FFN
                if f < 2:
                    what, i = f, 0
                elif n == N_SPLIT - 1:
                    what, i = 2, PAIRS - 1
                else:
                    i, what = divmod(f - 2, 3)
                    i += what < 2
                if what < 2:
                    at = what * D_FF + i * 256
                    c = tall(w["w_up"][l], every, slice(at, at + 256))
                else:
                    c = tall(w["w_down"][l], slice(i * 256, i * 256 + 256), every)
            chunks.append(c)
    return np.stack(chunks)


def _packs(w):
    out = np.empty((P, DEPTH, NV), np.float32)

    def put(l, at, v):
        cols = v.reshape(-1, P).T
        out[:, l, at:at + cols.shape[1]] = cols

    for l in range(DEPTH):
        put(l, V_G1, w["norm1_g"][l])
        put(l, V_G2, w["norm2_g"][l])
        put(l, V_CW, w["conv_w"][l])
        put(l, V_CB, w["conv_b"][l])
        put(l, V_LG, w["conv_ln_g"][l])
        put(l, V_LB, w["conv_ln_b"][l])
        put(l, V_QG, np.concatenate([w["q_norm_g"][l]] * 2))
        put(l, V_KG, np.concatenate([w["k_norm_g"][l]] * 2))
        put(l, V_FW, w["ffn_conv_w"][l])
        put(l, V_FB, w["ffn_conv_b"][l])
        for g, cols in enumerate(ADA_COLUMNS):
            put(l, V_AB + 4 * g, w["ada_b"][l][cols * 512:cols * 512 + 512])
    return out


def _onehot():
    hot = np.zeros((BUCKETS + 1, TABLE), np.float32)
    exact = BUCKETS // 2
    for i in range(TABLE):
        dist = i - (P - 1)
        if dist < 0:
            b = BUCKETS
        elif dist < exact:
            b = dist
        else:
            b = min(exact + int(math.log(dist / exact) / math.log(MAX_DISTANCE / exact) * (BUCKETS - exact)),
                    BUCKETS - 1)
        hot[b, i] = 1.0
    return hot


def kernel(**inputs):
    import concourse.bacc as bacc
    from concourse.bass_utils import run_bass_kernel_spmd

    w = {k: np.asarray(v) for k, v in inputs.items()}
    arrays = {
        "stream": _stream(w),
        "x": np.ascontiguousarray(w["x"][0].reshape(T, KD, P).transpose(2, 1, 0)),
        "c": np.ascontiguousarray(w["c"][0].reshape(KD, P).T),
        "packs": _packs(w),
        "rel": np.ascontiguousarray(w["rel_bias"].T),
        "onehot": _onehot(),
        "ident": np.eye(P, dtype=np.float32),
    }
    nc = bacc.Bacc("TRN2", target_bir_lowering=False, num_devices=1)
    args = [nc.dram_tensor(f"in_{n}", a.shape, F32, kind="ExternalInput").ap() for n, a in arrays.items()]
    out = nc.dram_tensor("out_x", (P, KD, T), F32, kind="ExternalOutput").ap()
    trunk(nc, *args, out)
    r = run_bass_kernel_spmd(nc, [{f"in_{n}": a for n, a in arrays.items()}], core_ids=[0])
    got = r.results[0]["out_x"]
    return got.transpose(2, 1, 0).reshape(1, T, D)
```
